# Optimizing a Trainium2 kernel written in Bass

```python
import jax, jax.numpy as jnp
from jax import lax
import numpy as np

D_MODEL = 1024
BATCH = 1
SEQ = 256
DEPTH = 2

GRID_W = 64
CTX_LEN = 256
N_MIXERS = 2
N_SSD_LAYERS = (DEPTH + 1) // 2
N_ATTN_LAYERS = DEPTH // 2
EPS = 1e-6

SSM_EXPAND = 2
D_INNER = SSM_EXPAND * D_MODEL
SSM_HEADDIM = 64
SSM_HEADS = D_INNER // SSM_HEADDIM
SSM_STATE = 128
SSM_GROUPS = 4
SSM_HPG = SSM_HEADS // SSM_GROUPS
SSM_CONV = 5
SSM_CHUNK = 128
GN = SSM_GROUPS * SSM_STATE
CONV_DIM = D_INNER + 2 * GN
D_IN_PROJ = 2 * D_INNER + 2 * GN + 2 * SSM_HEADS

HEAD_DIM = 64
N_Q_HEADS = D_MODEL // HEAD_DIM
N_KV_HEADS = 4
GQA_GROUP = N_Q_HEADS // N_KV_HEADS
WINDOW = 128
ATTN_BLOCK = 128
ROPE_BASE = 10000.0
ROPE_PAIRS = HEAD_DIM // 4
QKV_DIM = (N_Q_HEADS + 2 * N_KV_HEADS) * HEAD_DIM

N_EXPERTS = 16
N_EXPERT_GROUPS = 4
EXPERTS_PER_GROUP = N_EXPERTS // N_EXPERT_GROUPS
TOPK_GROUPS = 1
TOP_K = 2
D_EXPERT = 512
D_SHARED = 512

kernel_name = 'hybrid_ssd_swa_moe_dit_prefix'

def rmsnorm(x, w):
    xf = x.astype(jnp.float32)
    y = xf * lax.rsqrt(jnp.mean(xf * xf, axis=-1, keepdims=True) + EPS)
    return y.astype(x.dtype) * w

def modulate(x, shift, scale):
    return x * (1 + scale) + shift

def axial_rope_tables(rows):
    row = jnp.repeat(jnp.arange(rows), GRID_W)
    col = jnp.tile(jnp.arange(GRID_W), rows)
    inv_freq = ROPE_BASE ** (-jnp.arange(ROPE_PAIRS, dtype=jnp.float32) / ROPE_PAIRS)
    ang = jnp.stack([row, col], axis=-1).astype(jnp.float32)[:, :, None] * inv_freq
    return jnp.cos(ang), jnp.sin(ang)

def axial_rope(x, cos, sin):
    lead = x.shape[:-1]
    xr = x.reshape(lead + (2, 2, ROPE_PAIRS))
    bshape = (1, x.shape[1]) + (1,) * (x.ndim - 3) + (2, ROPE_PAIRS)
    c = cos.reshape(bshape).astype(x.dtype)
    s = sin.reshape(bshape).astype(x.dtype)
    x1, x2 = xr[..., 0, :], xr[..., 1, :]
    out = jnp.stack([x1 * c - x2 * s, x2 * c + x1 * s], axis=-2)
    return out.reshape(x.shape)

def centred_dwconv(u, w, b):
    pad = (SSM_CONV - 1) // 2
    y = lax.conv_general_dilated(u, w[:, None, :].astype(u.dtype), window_strides=(1,),
                                 padding=[(pad, pad)], dimension_numbers=('NWC', 'WIO', 'NWC'),
                                 feature_group_count=u.shape[-1])
    return y + b

def ssd_chunked_scan(xs, dt, a_neg, bm, cm, h0, need_y):
    f32 = jnp.float32
    bsz, L = xs.shape[0], xs.shape[1]
    nc = L // SSM_CHUNK
    x_c = xs.astype(f32).reshape(bsz, nc, SSM_CHUNK, SSM_GROUPS, SSM_HPG, SSM_HEADDIM)
    dt_c = dt.astype(f32).reshape(bsz, nc, SSM_CHUNK, SSM_GROUPS, SSM_HPG)
    b_c = bm.astype(f32).reshape(bsz, nc, SSM_CHUNK, SSM_GROUPS, SSM_STATE)
    c_c = cm.astype(f32).reshape(bsz, nc, SSM_CHUNK, SSM_GROUPS, SSM_STATE)
    cum = jnp.cumsum(dt_c * a_neg.astype(f32).reshape(SSM_GROUPS, SSM_HPG), axis=2)
    dtx = dt_c[..., None] * x_c
    decay_end = jnp.exp(cum[:, :, -1:] - cum)
    states = jnp.einsum('bcjgn,bcjgh,bcjghp->bcghpn', b_c, decay_end, dtx)
    chunk_decay = jnp.exp(cum[:, :, -1])

    def step(h, inp):
        st, dec = inp
        return h * dec[..., None, None] + st, h

    final, h_prev = lax.scan(step, h0.astype(f32),
                             (jnp.moveaxis(states, 1, 0), jnp.moveaxis(chunk_decay, 1, 0)))
    if not need_y:
        return None, final
    h_prev = jnp.moveaxis(h_prev, 0, 1)
    idx = jnp.arange(SSM_CHUNK)
    causal = (idx[:, None] >= idx[None, :])[None, None, :, :, None, None]
    seg = cum[:, :, :, None] - cum[:, :, None, :]
    decay_in = jnp.exp(jnp.where(causal, seg, -jnp.inf))
    cb = jnp.einsum('bcign,bcjgn->bcijg', c_c, b_c)
    y_diag = jnp.einsum('bcijg,bcijgh,bcjghp->bcighp', cb, decay_in, dtx)
    y_off = jnp.einsum('bcign,bcghpn,bcigh->bcighp', c_c, h_prev, jnp.exp(cum))
    y = (y_diag + y_off).reshape(bsz, L, SSM_HEADS, SSM_HEADDIM)
    return y.astype(xs.dtype), final

def ssd_mixer(h_lat, h_ctx, in_w, conv_w, conv_b, dt_bias, a_log, d_skip, norm_w, out_w, need_ctx_out):
    bsz = h_lat.shape[0]
    a_f = -jnp.exp(a_log[0])
    a_b = -jnp.exp(a_log[1])

    def project(h):
        L = h.shape[1]
        zxbcdt = h @ in_w
        z = zxbcdt[..., :D_INNER]
        xbc = jax.nn.silu(centred_dwconv(zxbcdt[..., D_INNER:D_INNER + CONV_DIM], conv_w, conv_b))
        dt_raw = zxbcdt[..., D_INNER + CONV_DIM:]
        xs = xbc[..., :D_INNER].reshape(bsz, L, SSM_HEADS, SSM_HEADDIM)
        bm = xbc[..., D_INNER:D_INNER + GN].reshape(bsz, L, SSM_GROUPS, SSM_STATE)
        cm = xbc[..., D_INNER + GN:].reshape(bsz, L, SSM_GROUPS, SSM_STATE)
        dt_f = jax.nn.softplus(dt_raw[..., :SSM_HEADS] + dt_bias[0])
        dt_b = jax.nn.softplus(dt_raw[..., SSM_HEADS:] + dt_bias[1])
        return z, xs, bm, cm, dt_f, dt_b

    def bidirectional(z, xs, bm, cm, dt_f, dt_b, h0_f, h0_b, need_y):
        L = xs.shape[1]
        y_f, fin_f = ssd_chunked_scan(xs, dt_f, a_f, bm, cm, h0_f, need_y)
        y_b, fin_b = ssd_chunked_scan(jnp.flip(xs, 1), jnp.flip(dt_b, 1), a_b,
                                      jnp.flip(bm, 1), jnp.flip(cm, 1), h0_b, need_y)
        if not need_y:
            return None, fin_f, fin_b
        y = y_f + jnp.flip(y_b, 1) + xs * d_skip[:, None]
        y = rmsnorm(y.reshape(bsz, L, D_INNER) * jax.nn.silu(z), norm_w)
        return y @ out_w, fin_f, fin_b

    zeros = jnp.zeros((bsz, SSM_GROUPS, SSM_HPG, SSM_HEADDIM, SSM_STATE), jnp.float32)
    out_c, fin_f, fin_b = bidirectional(*project(h_ctx), zeros, zeros, need_ctx_out)
    out_l, _, _ = bidirectional(*project(h_lat), fin_f, fin_b, True)
    return out_l, out_c

def attn_mixer(h_lat, h_ctx, qkv_w, sink, out_w, cos, sin, need_ctx_out):
    f32 = jnp.float32
    bsz, S = h_lat.shape[0], h_lat.shape[1]
    n_ctx = h_ctx.shape[1]
    nb = S // ATTN_BLOCK
    scale = HEAD_DIM ** -0.5
    qd = N_Q_HEADS * HEAD_DIM
    kd = N_KV_HEADS * HEAD_DIM

    def project(h):
        L = h.shape[1]
        qkv = h @ qkv_w
        q = qkv[..., :qd].reshape(bsz, L, N_KV_HEADS, GQA_GROUP, HEAD_DIM)
        k = qkv[..., qd:qd + kd].reshape(bsz, L, N_KV_HEADS, HEAD_DIM)
        v = qkv[..., qd + kd:].reshape(bsz, L, N_KV_HEADS, HEAD_DIM)
        return q, k, v

    q_c, k_c, v_c = project(h_ctx)
    q_l, k_l, v_l = project(h_lat)
    q_l = axial_rope(q_l, cos, sin)
    k_l = axial_rope(k_l, cos, sin)
    sink_b = sink.astype(f32).reshape(N_KV_HEADS, GQA_GROUP)[:, :, None, None]

    qb = q_l.reshape(bsz, nb, ATTN_BLOCK, N_KV_HEADS, GQA_GROUP, HEAD_DIM)
    pad = ((0, 0), (ATTN_BLOCK, ATTN_BLOCK), (0, 0), (0, 0))
    kp = jnp.pad(k_l, pad).reshape(bsz, nb + 2, ATTN_BLOCK, N_KV_HEADS, HEAD_DIM)
    vp = jnp.pad(v_l, pad).reshape(bsz, nb + 2, ATTN_BLOCK, N_KV_HEADS, HEAD_DIM)
    k_win = jnp.concatenate([kp[:, o:o + nb] for o in range(3)], axis=2)
    v_win = jnp.concatenate([vp[:, o:o + nb] for o in range(3)], axis=2)
    s_loc = jnp.einsum('bnqkgd,bnjkd->bnkgqj', qb, k_win).astype(f32) * scale
    s_ctx = jnp.einsum('bnqkgd,bckd->bnkgqc', qb, k_c).astype(f32) * scale
    blk = jnp.arange(nb)[:, None, None]
    qpos = blk * ATTN_BLOCK + jnp.arange(ATTN_BLOCK)[None, :, None]
    kpos = (blk - 1) * ATTN_BLOCK + jnp.arange(3 * ATTN_BLOCK)[None, None, :]
    valid = (jnp.abs(kpos - qpos) <= WINDOW) & (kpos >= 0) & (kpos < S)
    s_loc = jnp.where(valid[None, :, None, None], s_loc, -jnp.inf)
    sink_l = jnp.broadcast_to(sink_b, s_loc.shape[:-1] + (1,))
    p = jax.nn.softmax(jnp.concatenate([s_ctx, s_loc, sink_l], axis=-1), axis=-1).astype(v_l.dtype)
    p_ctx = p[..., :n_ctx]
    p_loc = p[..., n_ctx:n_ctx + 3 * ATTN_BLOCK]
    o = (jnp.einsum('bnkgqc,bckd->bnqkgd', p_ctx, v_c)
         + jnp.einsum('bnkgqj,bnjkd->bnqkgd', p_loc, v_win))
    out_l = o.reshape(bsz, S, qd) @ out_w

    out_c = None
    if need_ctx_out:
        s_cc = jnp.einsum('bqkgd,bckd->bkgqc', q_c, k_c).astype(f32) * scale
        sink_c = jnp.broadcast_to(sink_b, s_cc.shape[:-1] + (1,))
        p_c = jax.nn.softmax(jnp.concatenate([s_cc, sink_c], axis=-1), axis=-1)[..., :n_ctx]
        o_c = jnp.einsum('bkgqc,bckd->bqkgd', p_c.astype(v_c.dtype), v_c)
        out_c = o_c.reshape(bsz, n_ctx, qd) @ out_w
    return out_l, out_c

def swiglu(t, wg, wu, wd):
    return (jax.nn.silu(t @ wg) * (t @ wu)) @ wd

def grouped_moe(h, router_w, router_bias, w_gate, w_up, w_down, sh_gate, sh_up, sh_down):
    shp = h.shape
    t = h.reshape(-1, shp[-1])
    n_tok = t.shape[0]
    scores = jax.nn.sigmoid((t @ router_w).astype(jnp.float32))
    biased = (scores + router_bias.astype(jnp.float32)).reshape(n_tok, N_EXPERT_GROUPS, EXPERTS_PER_GROUP)
    group_score = lax.top_k(biased, TOP_K)[0].sum(-1)
    _, g_idx = lax.top_k(group_score, TOPK_GROUPS)
    g_mask = jax.nn.one_hot(g_idx, N_EXPERT_GROUPS, dtype=jnp.float32).sum(1) > 0
    cand = jnp.where(g_mask[:, :, None], biased, -jnp.inf).reshape(n_tok, N_EXPERTS)
    _, e_idx = lax.top_k(cand, TOP_K)
    w = jnp.take_along_axis(scores, e_idx, axis=-1)
    w = w / w.sum(-1, keepdims=True)
    combine = (jax.nn.one_hot(e_idx, N_EXPERTS, dtype=jnp.float32) * w[..., None]).sum(1).astype(t.dtype)
    out = swiglu(t, sh_gate, sh_up, sh_down)
    for e in range(N_EXPERTS):
        out = out + combine[:, e:e + 1] * swiglu(t, w_gate[e], w_up[e], w_down[e])
    return out.reshape(shp)

def setup_inputs(seed: int = 0) -> dict:
    key = jax.random.key(seed)
    ks = jax.random.split(key, 32)
    nrm = jax.random.normal
    D = D_MODEL
    dt0 = jnp.exp(jax.random.uniform(ks[10], (N_SSD_LAYERS, 2, SSM_HEADS),
                                     minval=np.log(1e-3), maxval=np.log(1e-1)))
    return {
        'x': nrm(ks[0], (BATCH, SEQ, D)),
        'c': nrm(ks[1], (BATCH, D)),
        'ctx': nrm(ks[2], (BATCH, CTX_LEN, D)),
        'c_ctx': nrm(ks[3], (D,)),
        'ada_w': nrm(ks[4], (DEPTH, D, 6 * D)) * (0.5 * D ** -0.5),
        'ada_b': nrm(ks[5], (DEPTH, 6 * D)) * 0.02,
        'norm1_w': 1.0 + 0.05 * nrm(ks[6], (DEPTH, D)),
        'norm2_w': 1.0 + 0.05 * nrm(ks[7], (DEPTH, D)),
        'ssd_in_w': nrm(ks[8], (N_SSD_LAYERS, D, D_IN_PROJ)) * D ** -0.5,
        'ssd_conv_w': nrm(ks[9], (N_SSD_LAYERS, SSM_CONV, CONV_DIM)) * SSM_CONV ** -0.5,
        'ssd_conv_b': nrm(ks[11], (N_SSD_LAYERS, CONV_DIM)) * 0.02,
        'ssd_dt_bias': dt0 + jnp.log(-jnp.expm1(-dt0)),
        'ssd_a_log': jnp.log(jax.random.uniform(ks[12], (N_SSD_LAYERS, 2, SSM_HEADS), minval=1.0, maxval=16.0)),
        'ssd_d': 1.0 + 0.1 * nrm(ks[13], (N_SSD_LAYERS, SSM_HEADS)),
        'ssd_norm_w': 1.0 + 0.05 * nrm(ks[14], (N_SSD_LAYERS, D_INNER)),
        'ssd_out_w': nrm(ks[15], (N_SSD_LAYERS, D_INNER, D)) * D_INNER ** -0.5,
        'attn_qkv_w': nrm(ks[16], (N_ATTN_LAYERS, D, QKV_DIM)) * D ** -0.5,
        'attn_sink': 0.5 * nrm(ks[17], (N_ATTN_LAYERS, N_Q_HEADS)),
        'attn_out_w': nrm(ks[18], (N_ATTN_LAYERS, N_Q_HEADS * HEAD_DIM, D)) * (N_Q_HEADS * HEAD_DIM) ** -0.5,
        'router_w': nrm(ks[19], (D, N_EXPERTS)) * D ** -0.5,
        'router_bias': 0.01 * nrm(ks[20], (N_EXPERTS,)),
        'moe_w_gate': nrm(ks[21], (DEPTH, N_EXPERTS, D, D_EXPERT)) * D ** -0.5,
        'moe_w_up': nrm(ks[22], (DEPTH, N_EXPERTS, D, D_EXPERT)) * D ** -0.5,
        'moe_w_down': nrm(ks[23], (DEPTH, N_EXPERTS, D_EXPERT, D)) * D_EXPERT ** -0.5,
        'shared_w_gate': nrm(ks[24], (DEPTH, D, D_SHARED)) * D ** -0.5,
        'shared_w_up': nrm(ks[25], (DEPTH, D, D_SHARED)) * D ** -0.5,
        'shared_w_down': nrm(ks[26], (DEPTH, D_SHARED, D)) * D_SHARED ** -0.5,
        'final_norm_w': 1.0 + 0.05 * nrm(ks[27], (D,)),
    }

def reference(x, c, ctx, c_ctx, ada_w, ada_b, norm1_w, norm2_w, ssd_in_w, ssd_conv_w, ssd_conv_b,
              ssd_dt_bias, ssd_a_log, ssd_d, ssd_norm_w, ssd_out_w, attn_qkv_w, attn_sink, attn_out_w,
              router_w, router_bias, moe_w_gate, moe_w_up, moe_w_down, shared_w_gate, shared_w_up,
              shared_w_down, final_norm_w):
    rows = x.shape[1] // GRID_W
    cos, sin = axial_rope_tables(rows)
    silu_c = jax.nn.silu(c)
    silu_cc = jax.nn.silu(c_ctx)
    h, hc = x, ctx
    for l in range(DEPTH):
        need_ctx_out = l < DEPTH - 1
        j = l // N_MIXERS
        sh1, sc1, g1, sh2, sc2, g2 = jnp.split((silu_c @ ada_w[l] + ada_b[l])[:, None, :], 6, axis=-1)
        csh1, csc1, cg1, csh2, csc2, cg2 = jnp.split(silu_cc @ ada_w[l] + ada_b[l], 6)
        a_l = modulate(rmsnorm(h, norm1_w[l]), sh1, sc1)
        a_c = modulate(rmsnorm(hc, norm1_w[l]), csh1, csc1)
        if l % N_MIXERS == 0:
            out_l, out_c = ssd_mixer(a_l, a_c, ssd_in_w[j], ssd_conv_w[j], ssd_conv_b[j], ssd_dt_bias[j],
                                     ssd_a_log[j], ssd_d[j], ssd_norm_w[j], ssd_out_w[j], need_ctx_out)
        else:
            out_l, out_c = attn_mixer(a_l, a_c, attn_qkv_w[j], attn_sink[j], attn_out_w[j], cos, sin, need_ctx_out)
        h = h + g1 * out_l
        m_l = modulate(rmsnorm(h, norm2_w[l]), sh2, sc2)
        h = h + g2 * grouped_moe(m_l, router_w, router_bias, moe_w_gate[l], moe_w_up[l], moe_w_down[l],
                                 shared_w_gate[l], shared_w_up[l], shared_w_down[l])
        if need_ctx_out:
            hc = hc + cg1 * out_c
            m_c = modulate(rmsnorm(hc, norm2_w[l]), csh2, csc2)
            hc = hc + cg2 * grouped_moe(m_c, router_w, router_bias, moe_w_gate[l], moe_w_up[l], moe_w_down[l],
                                        shared_w_gate[l], shared_w_up[l], shared_w_down[l])
    return rmsnorm(h, final_norm_w)


_drawn_inputs = setup_inputs


def setup_inputs(seed=0):
    import zlib

    import numpy as np

    out = dict(_drawn_inputs(seed))
    spreads = {}
    factors = {'ssd_conv_b': 3.089, 'attn_sink': 36.163}
    for name, (base, spread) in spreads.items():
        noise = np.random.default_rng([zlib.crc32(name.encode()), seed]).standard_normal(out[name].shape)
        drawn = base * np.exp(spread * noise) if base else spread * noise
        out[name] = __import__('jax').numpy.asarray(drawn.astype(out[name].dtype))
    for name, factor in factors.items():
        out[name] = (out[name] * factor).astype(out[name].dtype)
    return out
```

```python
from contextlib import ExitStack

import numpy as np

import concourse.bass as bass
from concourse import mybir

F32 = mybir.dt.float32
BF16 = mybir.dt.bfloat16
ALU = mybir.AluOpType
ACT = mybir.ActivationFunctionType
AX = mybir.AxisListType

P = 128
D = 1024
KD = D // P
S = 256
T = 2 * S
NT = T // P
EPS = 1e-6
DI = 2048
KI = DI // P
NH = 32
HP = 64
NG = 4
HG = NH // NG
GW = HG * HP
NCONV = (DI + 2 * NG * P) // P
TAPS = 5
PADS = (TAPS - 1) // 2
SEG = S + 2 * PADS
QH = 16
KVH = 4
HD = 64
SCALE = HD ** -0.5
WINDOW = 128
GRID_W = 64
NE = 16
FE = 512
KF = FE // P
NEG = -1e30

SLOTS = 6
SLOT = 2048
UC = 256
ADA_U = 6 * D // UC

XBC0 = DI
TILE_ORDER = [2, 3, 0, 1]


def host_constants():
    k = np.arange(P)
    ident = np.eye(P, dtype=np.float32)
    tri_f = (k[:, None] <= k[None, :]).astype(np.float32)
    tri_b = (k[:, None] >= k[None, :]).astype(np.float32)
    rope_m = np.zeros((P, P), np.float32)
    pairs = HD // 4
    for m in range(P):
        base, half = m - (m % (2 * pairs)), (m // pairs) % 2
        p = m % pairs
        if half == 0:
            rope_m[base + pairs + p, m] = -1.0
        else:
            rope_m[base + p, m] = 1.0
    tok = np.arange(S)
    pos = np.stack([tok // GRID_W, tok % GRID_W], axis=0).astype(np.float32)
    inv = (np.float32(10000.0) ** (-np.arange(pairs, dtype=np.float32) / np.float32(pairs))).astype(np.float32)
    axis = (k % HD) // (2 * pairs)
    ang = (pos[axis] * inv[k % pairs][:, None]).astype(np.float32)
    c32 = np.concatenate([ident, tri_f, tri_b, rope_m, np.cos(ang), np.sin(ang)], axis=1).astype(np.float32)
    mask_f = np.where(k[None, :] >= k[:, None], 0.0, NEG)
    mask_b = np.where(k[None, :] <= k[:, None], 0.0, NEG)
    am = []
    for b in range(S // P):
        diff = np.abs(np.arange(S)[None, :] - (b * P + k)[:, None])
        am += [np.where(diff <= WINDOW, 0.0, NEG), np.zeros((P, S))]
    c16 = np.concatenate([ident, mask_f, mask_b] + am, axis=1).astype(np.float32)
    erev = np.tile(np.concatenate([np.arange(NE, 0, -1), np.arange(4, 0, -1)]).astype(np.float32), (P, 1))
    return c32, c16, erev


class Unit:

    def __init__(self, index, parts, arrived):
        self.index, self.parts, self.slot, self.arrived = index, parts, index % SLOTS, arrived


def plan_units(kinds):
    counts = [0] * SLOTS
    units, index = {}, 0
    for name, n, parts in kinds:
        units[name] = []
        for _ in range(n):
            counts[index % SLOTS] += 16 * parts
            units[name].append(Unit(index, parts, counts[index % SLOTS]))
            index += 1
    return units


def build(nc, a, out):
    units = plan_units([("ada0", ADA_U, 1), ("xbc", NCONV // 2, 1), ("ada1", ADA_U, 1), ("z", DI // UC, 1),
                        ("out", KD, 1), ("moe0", (NE + 1) * 6, 1), ("q", 4, 1), ("k", 1, 1), ("v", 1, 1),
                        ("ao", D // UC, 1), ("moe1", (NE + 1) * 6, 1)])
    order = [(n, v) for n in ("ada0", "xbc", "ada1", "z", "out") for v in range(len(units[n]))]
    order1 = [(n, v) for n in ("q", "k", "v", "ao") for v in range(len(units[n]))]

    with ExitStack() as ctx:
        def sb(name, shape, dt=F32):
            return ctx.enter_context(nc.sbuf_tensor(name, shape, dt))

        def sem(name):
            return ctx.enter_context(nc.semaphore(name))

        ring = sb("ring", [P, SLOTS, SLOT])
        hT = sb("hT", [P, KD, T])
        aT = sb("aT", [P, KD, T])
        big = sb("big", [P, 8192])
        ssb = sb("ssb", [P, 10240])
        tmp = sb("tmp", [P, 8192])
        c32 = sb("c32", [P, 4 * P + 2 * S])
        c16 = sb("c16", [P, 3 * P + 2 * T], BF16)
        erev = sb("erev", [P, NE + 4])
        ones = sb("ones", [P, P])
        mean = sb("mean", [P, P])
        par = sb("par", [P, 312])
        cs = sb("cs", [P, 2, KD])
        mod = sb("mod", [P, 2, 48, 2])
        amod = sb("amod", [P, 2, 2, KD, 2])
        rstd = sb("rstd", [P, T])
        rw = sb("rw", [P, KD, NE])
        rb = sb("rb", [P, NE])
        sink = sb("sink", [P, QH])
        comb = sb("comb", [P, NT, NE])
        dtb = sb("dtb", [P, 64])
        expa = sb("expa", [P, 64])
        dskip = sb("dskip", [P, NH])
        dt = sb("dt", [P, NT, 64])
        cum = sb("cum", [P, NT, 64])
        ncum = sb("ncum", [P, NT, 64])
        ecum = sb("ecum", [P, NT, 64])
        wdt = sb("wdt", [P, NT, 64])
        cdec = sb("cdec", [P, NT, 64])
        cumT = sb("cumT", [64, T])
        small = sb("small", [P, 16])
        ps = ctx.enter_context(nc.psum_tensor("ps", [P, 8, 512], F32))

        ident, tri_f, tri_b = c32[:, 0:P], c32[:, P:2 * P], c32[:, 2 * P:3 * P]
        rope_m, cosT, sinT = c32[:, 3 * P:4 * P], c32[:, 4 * P:4 * P + S], c32[:, 4 * P + S:4 * P + 2 * S]
        identb = c16[:, 0:P]
        dmask = [c16[:, P:2 * P], c16[:, 2 * P:3 * P]]
        amask = [c16[:, 3 * P + b * T:3 * P + (b + 1) * T] for b in range(2)]

        xtok = big[:, 0:4096].rearrange("p (t n) -> p t n", t=NT)
        xs = big[:, :].rearrange("p (t n) -> p t n", t=NT)
        BT = ssb[:, 0:2048].rearrange("p (g n) -> p g n", g=NG)
        CT = ssb[:, 2048:4096].rearrange("p (g n) -> p g n", g=NG)
        BK = ssb[:, 4096:6144].rearrange("p (t n) -> p t n", t=NT)
        E = ssb[:, 6144:10240].rearrange("p (b h i) -> p b h i", b=2, h=16)
        wdtw = ssb[:, 6144:6656].rearrange("p (k n) -> p k n", k=KD)
        sp = [ssb[:, 6656 + 256 * n:6912 + 256 * n] for n in range(8)]
        c16f = tmp[:, 4096:4096 + 3 * P + 2 * T]
        packs = tmp[:, 0:384].rearrange("p (i n) -> p i n", i=3)
        pre = [tmp[:, 520 * n:520 * n + 520].rearrange("p (s n) -> p s n", s=2) for n in range(3)]
        cacc = [tmp[:, 1560 + 512 * n:2072 + 512 * n] for n in range(2)]
        xsT = [tmp[:, 2584 + 512 * n:3096 + 512 * n] for n in range(2)]
        dtx = [[tmp[:, 1024 * b + 512 * d:1024 * b + 512 * d + 512] for d in range(2)] for b in range(2)]
        wx = [tmp[:, 2048 + 512 * n:2560 + 512 * n] for n in range(2)]
        H = [[tmp[:, 3072 + 512 * (3 * d + n):3584 + 512 * (3 * d + n)] for n in range(3)] for d in range(2)]
        yb = [tmp[:, 6144 + 512 * n:6656 + 512 * n] for n in range(2)]
        cbs = [tmp[:, 7168 + 512 * n:7680 + 512 * n] for n in range(2)]
        yT = ssb[:, 0:8192].rearrange("p (k n) -> p k n", k=KI)
        junk = ssb[:, 8192:10240]
        sz = [tmp[:, 512 * n:512 * n + 512] for n in range(2)]
        acc = big[:, 0:4096].rearrange("p (t n) -> p t n", t=NT)
        hid = big[:, 4096:6144].rearrange("p (k n) -> p k n", k=KF)
        sg = [big[:, 6144 + 512 * n:6656 + 512 * n] for n in range(2)]
        rt = [tmp[:, 64 * n:64 * n + 64] for n in range(16)]
        QT = big[:, 0:2048].rearrange("p (c n) -> p c n", c=8)
        KT = big[:, 2048:3072].rearrange("p (c n) -> p c n", c=2)
        V = big[:, 3072:4096].rearrange("p (t n) -> p t n", t=NT)
        O = big[:, 4096:6144].rearrange("p (b n) -> p b n", b=2)
        oT = big[:, 6144:8192].rearrange("p (k n) -> p k n", k=8)
        rq = [ssb[:, 512 * n:512 * n + 512] for n in range(2)]
        pr = [ssb[:, 1024 + 512 * n:1536 + 512 * n] for n in range(2)]
        prT = [ssb[:, 2048 + 512 * n:2560 + 512 * n] for n in range(2)]
        KX = ssb[:, 5120:6144].rearrange("p (c n) -> p c n", c=2)
        rmx = ssb[:, 3072:3104]
        mxa = ssb[:, 3104:3136]
        nmx = ssb[:, 3136:3168]
        den = ssb[:, 3168:3200]
        esk = ssb[:, 3200:3232]
        rden = ssb[:, 3232:3264]
        fnw = ssb[:, 4096:5120]
        fin = ssb[:, 6144:8192].rearrange("p (t n) -> p t n", t=2)
        fsq = ssb[:, 8192:9216]

        n_consts, n_packs, n_x, n_bc = 3, 9, 2, 5
        s_const, s_pack, s_x, s_bc = sem("consts_in"), sem("packs_in"), sem("x_in"), sem("rows_in")
        s_set = sem("memsets")
        s_w = [sem(f"unit_in{n}") for n in range(SLOTS)]
        s_pkT, s_par, s_cs = sem("packs_turned"), sem("params_ready"), sem("silu_c")
        s_xT, s_hd, s_ha = sem("x_turned"), sem("hT_by_dve"), sem("hT_by_act")
        s_ada, s_mod = sem("ada_units"), sem("mod_ready")
        s_sq, s_ms, s_rv, s_rs, s_nx, s_a = (sem("squares"), sem("mean_square"), sem("recip_ms"), sem("rstd_ready"),
                                             sem("normed"), sem("modulated"))
        s_ip, s_pre, s_conv, s_sil = sem("in_proj"), sem("conv_input"), sem("conv_done"), sem("conv_silu")
        s_tr, s_trev = sem("xbc_turned"), sem("xbc_tokens")
        s_dt, s_sp, s_dA, s_cum, s_cumv, s_exps = (sem("dt_raw"), sem("softplus_steps"), sem("dA_ready"),
                                                   sem("cum_ready"), sem("cum_copied"), sem("decays"))
        s_spe = sem("softplus_exp")
        s_wdt, s_cT, s_cTv = sem("wdt_ready"), sem("cum_turned"), sem("cumT_ready")
        s_v = sem("dve_chain")
        s_b4, s_b4v, s_wx = sem("cb_or_state"), sem("cb_or_state_taken"), sem("weighted_x")
        s_R, s_E, s_M, s_dtx = sem("cum_rows"), sem("decay_matrices"), sem("mixed_matrices"), sem("dt_x")
        s_off, s_Y, s_yo, s_pl, s_y = (sem("y_off"), sem("y_diag"), sem("y_summed"), sem("pool_chain"), sem("y_done"))
        s_z, s_sz, s_zy = sem("z_proj"), sem("silu_z"), sem("gated")
        s_ss, s_ry, s_rq, s_yn = sem("y_square_sum"), sem("y_recip"), sem("y_rstd"), sem("y_normed")
        s_yt, s_ytd, s_yta = sem("y_turned"), sem("yT_by_dve"), sem("yT_by_act")
        s_op, s_h1 = sem("out_proj"), sem("h_plus_mixer")
        s_rl, s_rs1, s_cmb = sem("router_logits"), sem("router_sigmoid"), sem("combine_ready")
        s_gu, s_sg, s_hid, s_gf, s_y4, s_yn4, s_yu = (sem("gate_up"), sem("silu_gate"), sem("hidden"), sem("gate_unit"),
                                                      sem("down_unit"), sem("expert_out"), sem("expert_out_used"))
        s_mt, s_h2 = sem("moe_turned"), sem("h_plus_moe")
        s_q, s_qc, s_rot, s_ro1, s_rp = (sem("q_units"), sem("qk_copied"), sem("rotated"), sem("rope_cos"),
                                         sem("rope_done"))
        s_kx = sem("keys_exchanged")
        s_kv, s_vv, s_kc = sem("kv_units"), sem("v_copied"), sem("k_copied")
        s_sc, s_mx, s_p, s_pt, s_ptv, s_pv = (sem("scores"), sem("row_max"), sem("probs"), sem("probs_turned"),
                                              sem("probsT"), sem("pv"))
        s_es0, s_esk, s_o, s_ot, s_otv, s_ao = sem("sink_minus_max"), sem("sink_exp"), sem("o_ready"), sem("o_turned"), sem("oT_ready"), sem("attn_out")
        s_ft, s_fc, s_fs, s_fr, s_fq, s_fo, s_fw, s_fin = (sem("final_turned"), sem("final_copied"), sem("final_square"),
                                                     sem("final_recip"), sem("final_rstd"), sem("final_ready"),
                                                     sem("final_w_in"), sem("out_written"))

        NOUT = [2 * NT, NT]
        TOK = [T, S]
        GU0 = [0, (NE + 1) * KF]
        Y0 = [0, (NE + 1) * NOUT[0]]

        def unit_free(name, v):
            return {"ada0": (s_ada, v + 1), "ada1": (s_ada, ADA_U + v + 1), "xbc": (s_ip, 2 * (v + 1)),
                    "z": (s_z, 2 * (v + 1)), "out": (s_op, v + 1), "q": (s_q, v + 1), "k": (s_kv, 1),
                    "v": (s_kv, 3), "ao": (s_ao, 2 * (v + 1))}[name]

        def expert_free(l, n, j):
            e = (NE + 1) * l + n
            if j in (0, 2):
                return s_gf, 2 * e + 1 + j // 2
            if j in (1, 3):
                return s_gu, GU0[l] + KF * n + j + 1
            if j == 4:
                return s_y4, e + 1
            return s_yn4, Y0[l] + NOUT[l] * (n + 1)

        def cols(w, c0, width):
            return w[:, c0:c0 + width].rearrange("(k p) n -> p k n", p=P)

        def unit_source(name, v):
            if name in ("ada0", "ada1"):
                return cols(a["ada_w"][int(name[3])], v * UC, UC)
            if name == "xbc":
                c0 = XBC0 + DI + v * UC if v < 4 else XBC0 + (v - 4) * UC
                return cols(a["ssd_in_w"][0], c0, UC)
            if name == "z":
                return cols(a["ssd_in_w"][0], v * UC, UC)
            if name == "out":
                return cols(a["ssd_out_w"][0], v * P, P)
            if name == "q":
                return cols(a["attn_qkv_w"][0], v * UC, UC)
            if name == "k":
                return cols(a["attn_qkv_w"][0], QH * HD, UC)
            if name == "v":
                return cols(a["attn_qkv_w"][0], QH * HD + KVH * HD, UC)
            if name == "ao":
                return cols(a["attn_out_w"][0], v * UC, UC)

        def slot(u, k=KD):
            return ring[:, u.slot, :].rearrange("p (k n) -> p k n", k=k)

        def arrived(eng, u, n=0):
            eng.wait_ge(s_w[u.slot], u.arrived + n * 16)

        block = ctx.enter_context(nc.Block())

        @block.sync
        def _(sp_):
            sp_.dma_start(c32[:, :], a["c32"]).then_inc(s_const, 16)
            sp_.dma_start(c16f, a["c16"]).then_inc(s_const, 16)
            sp_.dma_start(erev[:, :], a["erev"]).then_inc(s_const, 16)
            packed = [(0, 0, a["ssd_conv_w"][0].rearrange("t (c p) -> (t c) p", p=P)),
                      (0, 120, a["final_norm_w"].rearrange("(c p) -> c p", p=P)),
                      (1, 0, a["ada_b"].rearrange("l (c p) -> (l c) p", p=P)),
                      (1, 96, a["norm1_w"].rearrange("l (c p) -> (l c) p", p=P)),
                      (1, 112, a["norm2_w"].rearrange("l (c p) -> (l c) p", p=P)),
                      (2, 0, a["ssd_norm_w"].rearrange("l (c p) -> (l c) p", p=P)),
                      (2, 16, a["ssd_conv_b"].rearrange("l (c p) -> (l c) p", p=P)),
                      (2, 40, a["c"].rearrange("l (c p) -> (l c) p", p=P)),
                      (2, 48, a["c_ctx"].rearrange("(c p) -> c p", p=P))]
            for i, r, src in packed:
                sp_.dma_start(packs[r:r + src.shape[0], i, :], src).then_inc(s_pack, 16)
            sp_.dma_start(xtok[:, 0:2, :], a["x"][0].rearrange("(t p) n -> p t n", p=P)).then_inc(s_x, 16)
            sp_.dma_start(xtok[:, 2:4, :], a["ctx"][0].rearrange("(t p) n -> p t n", p=P)).then_inc(s_x, 16)

            events = []

            def load(name, v):
                u = units[name][v]
                if u.index >= SLOTS:
                    s, n = events[u.index - SLOTS]
                    sp_.wait_ge(s, n)
                sp_.dma_start(slot(u, KI if name == "out" else KD), unit_source(name, v)).then_inc(s_w[u.slot], 16)
                events.append(unit_free(name, v))

            def expert_units(l, n, gate, up, down):
                for j in range(6):
                    u = units[f"moe{l}"][j]
                    if not isinstance(n, int):
                        s, c = expert_free(l, n - 1, j)
                        sp_.wait_ge(s, c)
                    else:
                        s, c = events[u.index - SLOTS]
                        sp_.wait_ge(s, c)
                    h = j // 2
                    if j < 4:
                        src = (gate, up)[j % 2][:, h * UC:(h + 1) * UC].rearrange("(k p) n -> p k n", p=P)
                        dst = slot(u)
                    else:
                        src = down[(j - 4) * 2 * P:(j - 3) * 2 * P, :].rearrange("(k p) n -> p k n", p=P)
                        dst = slot(u, 2)
                    sp_.dma_start(dst, src).then_inc(s_w[u.slot], 16)

            def moe(l):
                expert_units(l, 0, a["shared_w_gate"][l], a["shared_w_up"][l], a["shared_w_down"][l])
                with sp_.Fori(0, NE) as e:
                    one = bass.ds(e, 1)
                    expert_units(l, e + 1, a["moe_w_gate"][l, one].rearrange("o k n -> (o k) n"),
                                 a["moe_w_up"][l, one].rearrange("o k n -> (o k) n"),
                                 a["moe_w_down"][l, one].rearrange("o k n -> (o k) n"))
                for n in range(NE + 1):
                    events.extend(expert_free(l, n, j) for j in range(6))

            for name, v in order:
                load(name, v)
            moe(0)
            for name, v in order1:
                load(name, v)
            moe(1)
            for t in range(2):
                sp_.wait_ge(s_fo, t + 1)
                sp_.dma_start(out[0, t * P:(t + 1) * P, :], fin[:, t, :]).then_inc(s_fin, 16)
            sp_.wait_ge(s_fin, 32)

        @block.gpsimd
        def _(pool):
            pool.memset(ones[:, :], 1.0).then_inc(s_set, 1)
            pool.memset(mean[:, :], 1.0 / D).then_inc(s_set, 1)
            pool.wait_ge(s_const, 16 * n_consts)
            pool.tensor_copy(c16[:, :], c16f).then_inc(s_set, 1)
            pool.wait_ge(s_pkT, 1)
            for n in range(3):
                pool.memset(pre[n][:, :, 0:PADS], 0.0).then_inc(s_set, 1)
                pool.memset(pre[n][:, :, PADS + S:SEG], 0.0).then_inc(s_set, 1)

            def heads(v, col):
                return v[:, col:col + HG].unsqueeze(2).to_broadcast([P, HG, HP])

            def per_head(v):
                return v.rearrange("p (h n) -> p h n", h=HG)

            pool.wait_ge(s_trev, 20)
            pool.wait_ge(s_wdt, 1)
            for g in range(NG):
                cg = slice(g * GW, (g + 1) * GW)
                for q, (d, t) in enumerate([(0, 2), (1, 3), (0, 3), (1, 2), (0, 0), (1, 1)]):
                    n = 6 * g + q
                    if n >= 2:
                        pool.wait_ge(s_b4, 7 * ((n - 2) // 6) + (n - 2) % 6 + 2)
                    pool.tensor_tensor(per_head(wx[n % 2]), per_head(xs[:, t, cg]), heads(wdt[:, t, :], d * NH + g * HG),
                                       ALU.mult).then_inc(s_wx, 1)
                for i, t in enumerate(TILE_ORDER):
                    s = 4 * g + i
                    if s >= 2:
                        pool.wait_ge(s_Y, s - 1)
                    for d in range(2):
                        pool.tensor_tensor(per_head(dtx[s % 2][d]), per_head(xs[:, t, cg]),
                                           heads(dt[:, t, :], d * NH + g * HG), ALU.mult).then_inc(s_dtx, 1)
                    pool.wait_ge(s_dtx, 2 * s + 2)
                    pool.tensor_tensor(per_head(xs[:, t, cg]), per_head(xs[:, t, cg]), heads(dskip[:, :], g * HG),
                                       ALU.mult).then_inc(s_pl, 1)
                    pool.wait_ge(s_pl, s + 1)
                    pool.wait_ge(s_yo, s + 1)
                    pool.tensor_tensor(xs[:, t, cg], xs[:, t, cg], yb[s % 2], ALU.add).then_inc(s_y, 1)

        @block.scalar
        def _(act):
            act.dma_start(wdtw, a["ssd_in_w"][0][:, DI + NCONV * P:DI + NCONV * P + 64].rearrange("(k p) n -> p k n", p=P))\
                .then_inc(s_bc, 16)
            act.dma_start(rw[:, :, :], a["router_w"].rearrange("(k p) n -> p k n", p=P)).then_inc(s_bc, 16)
            rows = [(dtb[:, :], a["ssd_dt_bias"].rearrange("l d h -> (l d h)")),
                    (expa[:, :], a["ssd_a_log"].rearrange("l d h -> (l d h)")),
                    (dskip[:, :], a["ssd_d"].rearrange("l h -> (l h)")),
                    (rb[:, :], a["router_bias"]), (sink[:, :], a["attn_sink"].rearrange("l h -> (l h)"))]
            for dst, src in rows:
                act.dma_start(dst, src.partition_broadcast(P)).then_inc(s_bc, 16)

            act.wait_ge(s_par, 1)
            act.activation(cs[:, :, :], par[:, 296:312].rearrange("p (c k) -> p c k", c=2), ACT.Silu).then_inc(s_cs, 1)
            for k in range(1, KD, 2):
                act.wait_ge(s_xT, k + 1)
                act.copy(hT[:, k, :], ps[:, (k + 1) % 8, :]).then_inc(s_ha, 1)

            def norm_modulate(l, m, n, ready):
                i = 2 * l + m
                for k in range(KD):
                    ready(k)
                    act.activation(aT[:, k, 0:n], hT[:, k, 0:n], ACT.Square).then_inc(s_sq, 1)
                act.wait_ge(s_rv, i + 1)
                act.activation(rstd[:, 0:n], rstd[:, 0:n], ACT.Sqrt).then_inc(s_rs, 1)
                if i == 0:
                    act.wait_ge(s_mod, 3)
                elif l == 1 and m == 0:
                    act.wait_ge(s_mod, 6)
                for k in range(KD):
                    act.wait_ge(s_nx, KD * i + k + 1)
                    for q in range(n // S):
                        ins = act.activation(aT[:, k, q * S:(q + 1) * S], aT[:, k, q * S:(q + 1) * S], ACT.Identity,
                                             bias=mod[:, l, 24 * m + k, q:q + 1], scale=amod[:, l, m, k, q:q + 1])
                    ins.then_inc(s_a, 1)

            def ready0(k):
                if k % 2:
                    act.wait_ge(s_ha, k // 2 + 1)
                else:
                    act.wait_ge(s_hd, k // 2 + 1)

            norm_modulate(0, 0, T, ready0)

            act.wait_ge(s_sp, 2)
            act.activation(sp[1], sp[1], ACT.Exp, scale=-1.0).then_inc(s_spe, 1)
            act.wait_ge(s_bc, 16 * 7)
            act.activation(expa[:, :], expa[:, :], ACT.Exp).then_inc(s_spe, 1)

            def decays():
                act.wait_ge(s_cumv, 4)
                act.activation(ecum[:, :, :], cum[:, :, :], ACT.Exp).then_inc(s_exps, 1)
                act.activation(cdec[:, :, :], cdec[:, :, :], ACT.Exp).then_inc(s_exps, 1)
                act.activation(wdt[:, :, :], wdt[:, :, :], ACT.Exp).then_inc(s_exps, 1)

            def conv_in(i):
                act.wait_ge(s_ip, i + 1)
                if i >= 3:
                    act.wait_ge(s_conv, i - 2)
                else:
                    act.wait_ge(s_set, 9)
                act.copy(pre[i % 3][:, :, PADS:PADS + S], ps[:, i % 3, :].rearrange("p (s n) -> p s n", s=2))\
                    .then_inc(s_pre, 1)

            def conv_silu(i):
                act.wait_ge(s_conv, i + 1)
                if i < 4:
                    dst = BT[:, i, :]
                elif i < 8:
                    dst = CT[:, i - 4, :]
                else:
                    dst = xsT[i % 2]
                    if i >= 10:
                        act.wait_ge(s_tr, i - 5)
                act.activation(dst, cacc[i % 2], ACT.Silu).then_inc(s_sil, 1)

            def tokens(i):
                if 4 <= i < 8:
                    return
                j = i if i < 4 else i - 4
                act.wait_ge(s_tr, j + 1)
                src = ps[:, 3 + j % 2, :].rearrange("p (t n) -> p t n", t=NT)
                dst = BK[:, :, i * P:(i + 1) * P] if i < 4 else xs[:, :, (i - 8) * P:(i - 7) * P]
                act.copy(dst, src).then_inc(s_trev, 1)

            for i in range(NCONV + 3):
                if i < NCONV:
                    conv_in(i)
                if 0 <= i - 1 < NCONV:
                    conv_silu(i - 1)
                if 0 <= i - 3 < NCONV:
                    tokens(i - 3)
            decays()

            for s in range(4 * NG):
                g, t = s // 4, TILE_ORDER[s % 4]
                if s >= 2:
                    act.wait_ge(s_Y, s - 1)
                for q in range(4):
                    act.wait_ge(s_R, 4 * s + q + 1)
                    for j in range(4):
                        h = 4 * q + j
                        col = (h // HG) * NH + g * HG + h % HG
                        ins = act.activation(E[:, s % 2, h, :], ps[:, q, j * P:(j + 1) * P], ACT.Exp,
                                             bias=ncum[:, t, col:col + 1])
                    ins.then_inc(s_E, 1)

            for b in range(16):
                act.wait_ge(s_z, b + 1)
                if b >= 2:
                    act.wait_ge(s_zy, b - 1)
                act.activation(sz[b % 2], ps[:, b % 4, :], ACT.Silu).then_inc(s_sz, 1)
            act.wait_ge(s_zy, 16)
            for t in range(NT):
                act.activation(junk, xs[:, t, :], ACT.Square, accum_out=small[:, t:t + 1]).then_inc(s_ss, 1)
                act.wait_ge(s_ss, t + 1)
            act.wait_ge(s_ry, 1)
            act.activation(small[:, 8:12], small[:, 4:8], ACT.Sqrt).then_inc(s_rq, 1)
            for k in range(1, KI, 2):
                act.wait_ge(s_yt, k + 1)
                act.activation(yT[:, k, :], ps[:, 4 + k % 4, :], ACT.Copy, scale=par[:, 256 + k:257 + k]).then_inc(s_yta, 1)

            def moe_act(l, n0):
                n = TOK[l]

                def expert(e):
                    for f in range(KF):
                        q = KF * e + f
                        act.wait_ge(s_gu, GU0[l] + q + 1)
                        if not (isinstance(e, int) and q < 2):
                            act.wait_ge(s_hid, GU0[l] + q - 1)
                        act.activation(sg[f % 2][:, 0:n], ps[:, 2 * (f % 2), 0:n], ACT.Silu).then_inc(s_sg, 1)

                act.wait_ge(s_rl, l + 1)
                act.activation(rt[0][:, 0:n // P * NE], ps[:, 6, 0:n // P * NE], ACT.Sigmoid).then_inc(s_rs1, 1)
                expert(0)
                with act.Fori(0, NE) as e:
                    expert(e + 1)

            norm_modulate(0, 1, T, lambda k: act.wait_ge(s_h1, k + 1))
            moe_act(0, T)

            norm_modulate(1, 0, T, lambda k: act.wait_ge(s_h2, k + 1))
            for c in range(4):
                act.wait_ge(s_q, c + 1)
                act.copy(QT[:, 2 * c:2 * c + 2, :], ps[:, c, :].rearrange("p (c n) -> p c n", c=2)).then_inc(s_qc, 1)
            act.wait_ge(s_kv, 1)
            for m in range(2):
                act.copy(KT[:, m, :], ps[:, 4 + m, :]).then_inc(s_kc, 1)
            for c in range(2):
                act.wait_ge(s_kv, 2 + c)
                act.copy(V[:, 2 * c:2 * c + 2, :], ps[:, 6 + c, :].rearrange("p (c n) -> p c n", c=2)).then_inc(s_vv, 1)

            act.wait_ge(s_rp, 5)
            for w in range(2):
                act.dma_start(KX[(1 - w) * HD:(2 - w) * HD, :, :], KT[w * HD:(w + 1) * HD, :, :]).then_inc(s_kx, 16)

            def probs(n):
                act.wait_ge(s_mx, 3 * n + 3)
                if n >= 2:
                    act.wait_ge(s_pt, n - 1)
                act.activation(pr[n % 2], ps[:, n % 2, :], ACT.Exp, bias=nmx[:, n:n + 1], scale=SCALE,
                               accum_out=den[:, n:n + 1]).then_inc(s_p, 1)

            def turned(n):
                act.wait_ge(s_pt, n + 1)
                if n >= 2:
                    act.wait_ge(s_pv, n - 1)
                act.copy(prT[n % 2], ps[:, 2 + n % 2, :]).then_inc(s_ptv, 1)

            for n in range(33):
                if n < 32:
                    probs(n)
                if n >= 1:
                    turned(n - 1)
            act.wait_ge(s_es0, 1)
            act.activation(esk, esk, ACT.Exp).then_inc(s_esk, 1)
            act.dma_start(fnw, a["final_norm_w"].partition_broadcast(P)).then_inc(s_fw, 16)
            norm_modulate(1, 1, S, lambda k: act.wait_ge(s_h1, KD + k + 1))
            moe_act(1, S)

            for t in range(2):
                act.wait_ge(s_fc, 2 * (t + 1))
                if t:
                    act.wait_ge(s_fs, 1)
                act.activation(fsq, fin[:, t, :], ACT.Square, accum_out=small[:, t:t + 1]).then_inc(s_fs, 1)
            act.wait_ge(s_fr, 1)
            act.activation(small[:, 4:6], small[:, 2:4], ACT.Sqrt).then_inc(s_fq, 1)

        @block.tensor
        def _(pe):
            pe.wait_ge(s_const, 16 * n_consts)
            pe.wait_ge(s_pack, 16 * n_packs)
            for i, rows in enumerate((P, P, 56)):
                ins = pe.transpose(ps[:, 0, i * P:i * P + rows], packs[0:rows, i, :], ident[0:rows, 0:rows])
            ins.then_inc(s_pkT, 1)
            pe.wait_ge(s_x, 32)
            for k in range(KD):
                if k == 7:
                    pe.wait_ge(s_par, 1)
                for t in range(NT):
                    ins = pe.transpose(ps[:, (k + 1) % 8, t * P:(t + 1) * P], xtok[:, t, k * P:(k + 1) * P], ident)
                ins.then_inc(s_xT, 1)

            def ada(l, bank):
                for v, u in enumerate(units[f"ada{l}"]):
                    arrived(pe, u)
                    w = slot(u)
                    for c in range(2):
                        j = 2 * (2 * v + c)
                        for k in range(KD):
                            ins = pe.matmul(ps[:, bank, j:j + 2], w[:, k, c * P:(c + 1) * P], cs[:, :, k],
                                            start=(k == 0), stop=(k == KD - 1))
                    ins.then_inc(s_ada, 1)

            def mean_square(i, n, bank):
                for k in range(KD):
                    pe.wait_ge(s_sq, KD * i + k + 1)
                    ins = pe.matmul(ps[:, bank, 0:n], mean[:, :], aT[:, k, 0:n], start=(k == 0), stop=(k == KD - 1))
                ins.then_inc(s_ms, 1)

            pe.wait_ge(s_set, 2)
            pe.wait_ge(s_hd, 4)
            pe.wait_ge(s_ha, 4)
            mean_square(0, T, 7)
            pe.wait_ge(s_cs, 1)
            ada(0, 1)

            pe.wait_ge(s_bc, 16 * 7)
            pe.wait_ge(s_a, KD)
            for t in range(NT):
                for k in range(KD):
                    ins = pe.matmul(ps[:, 5, t * 64:(t + 1) * 64], aT[:, k, t * P:(t + 1) * P], wdtw[:, k, :],
                                    start=(k == 0), stop=(k == KD - 1))
            ins.then_inc(s_dt, 1)

            def turn_chunk(i):
                if 4 <= i < 8:
                    return
                j = i if i < 4 else i - 4
                pe.wait_ge(s_sil, i + 1)
                if j >= 2:
                    pe.wait_ge(s_trev, j - 1)
                src = BT[:, i, :] if i < 4 else xsT[i % 2]
                for t in range(NT):
                    ins = pe.transpose(ps[:, 3 + j % 2, t * P:(t + 1) * P], src[:, t * P:(t + 1) * P], ident)
                ins.then_inc(s_tr, 1)

            for i in range(NCONV + 2):
                if i < NCONV:
                    u = units["xbc"][i // 2]
                    arrived(pe, u)
                    if i == 1:
                        pe.wait_ge(s_mod, 1)
                    if i >= 3:
                        pe.wait_ge(s_pre, i - 2)
                    w = slot(u)
                    for k in range(KD):
                        ins = pe.matmul(ps[:, i % 3, :], w[:, k, (i % 2) * P:(i % 2 + 1) * P], aT[:, k, :],
                                        start=(k == 0), stop=(k == KD - 1))
                    ins.then_inc(s_ip, 1)
                if i >= 2:
                    turn_chunk(i - 2)
                if i == 6:
                    pe.wait_ge(s_dA, 1)
                    for t in range(NT):
                        pe.matmul(ps[:, 6, t * 64:t * 64 + 32], tri_f, sp[6][:, t * 64:t * 64 + 32], start=True, stop=True)
                        pe.matmul(ps[:, 6, t * 64 + 32:t * 64 + 64], tri_b, sp[6][:, t * 64 + 32:t * 64 + 64],
                                  start=True, stop=True)
                    pe.matmul(ps[:, 7, 0:256], ones[:, :], sp[6], start=True, stop=True).then_inc(s_cum, 1)
                if i == 10:
                    pe.wait_ge(s_cumv, 1)
                    for t in range(NT):
                        ins = pe.transpose(ps[0:64, 5, t * P:(t + 1) * P], cum[:, t, :], ident)
                    ins.then_inc(s_cT, 1)

            pe.wait_ge(s_pre, NCONV)
            ada(1, 0)

            def cb(g):
                if g:
                    pe.wait_ge(s_b4v, 7 * g)
                else:
                    pe.wait_ge(s_trev, 20)
                for t in range(NT):
                    ins = pe.matmul(ps[:, 4, t * P:(t + 1) * P], BT[:, g, t * P:(t + 1) * P],
                                    CT[:, g, t * P:(t + 1) * P], start=True, stop=True)
                ins.then_inc(s_b4, 1)

            def states(g):
                for q, (d, t) in enumerate([(0, 2), (1, 3), (0, 3), (1, 2), (0, 0), (1, 1)]):
                    pe.wait_ge(s_b4v, 7 * g + q + 1)
                    pe.wait_ge(s_wx, 6 * g + q + 1)
                    pe.matmul(ps[:, 4, :], BK[:, t, g * P:(g + 1) * P], wx[q % 2], start=True, stop=True).then_inc(s_b4, 1)

            def cum_rows(s):
                g, t = s // 4, TILE_ORDER[s % 4]
                for q in range(4):
                    if s:
                        pe.wait_ge(s_E, 4 * (s - 1) + q + 1)
                    d = q // 2
                    bank = ps[:, q, :].rearrange("p (h i) -> p h i", h=4)
                    pe.matmul(bank, identb, dmask[d].unsqueeze(1).to_broadcast([P, 4, P]), start=True, stop=False,
                              skip_group_check=True)
                    for j in range(4):
                        h = 4 * q + j
                        col = d * NH + g * HG + h % HG
                        ins = pe.matmul(bank[:, j, :], ident[0:64, col:col + 1].to_broadcast([64, P]),
                                        cumT[:, t * P:(t + 1) * P], start=False, stop=(j == 3), skip_group_check=True)
                    ins.then_inc(s_R, 1)

            def y_off(s):
                g, t = s // 4, TILE_ORDER[s % 4]
                if s:
                    pe.wait_ge(s_yo, s)
                pe.wait_ge(s_b4v, 7 * g + 7)
                lhs = CT[:, g, t * P:(t + 1) * P]
                if t != 2:
                    ins = pe.matmul(ps[:, 6, :], lhs, H[0][{3: 0, 0: 1, 1: 2}[t]], start=True, stop=True)
                if t != 3:
                    ins = pe.matmul(ps[:, 7, :], lhs, H[1][{2: 0, 1: 1, 0: 2}[t]], start=True, stop=True)
                ins.then_inc(s_off, 1)

            def y_diag(s):
                pe.wait_ge(s_dtx, 2 * s + 2)
                pe.wait_ge(s_M, 2 * s + 2)
                for h in range(HG):
                    for d in range(2):
                        ins = pe.matmul(ps[:, 5, h * HP:(h + 1) * HP], E[:, s % 2, d * HG + h, :],
                                        dtx[s % 2][d][:, h * HP:(h + 1) * HP], start=(d == 0), stop=(d == 1))
                ins.then_inc(s_Y, 1)

            pe.wait_ge(s_set, 9)
            pe.wait_ge(s_mod, 4)
            pe.wait_ge(s_cTv, 1)
            pe.wait_ge(s_exps, 3)
            cb(0)
            states(0)
            cum_rows(0)
            for s in range(4 * NG):
                if s + 1 < 4 * NG:
                    cum_rows(s + 1)
                y_off(s)
                y_diag(s)
                if s % 4 == 3 and s // 4 + 1 < NG:
                    cb(s // 4 + 1)
                    states(s // 4 + 1)

            pe.wait_ge(s_E, 16 * NG)
            for b in range(16):
                u = units["z"][b // 2]
                arrived(pe, u)
                if b >= 4:
                    pe.wait_ge(s_sz, b - 3)
                w = slot(u)
                for i in range(2):
                    t = 2 * (b % 2) + i
                    for k in range(KD):
                        ins = pe.matmul(ps[:, b % 4, i * UC:(i + 1) * UC], aT[:, k, t * P:(t + 1) * P], w[:, k, :],
                                        start=(k == 0), stop=(k == KD - 1))
                ins.then_inc(s_z, 1)

            pe.wait_ge(s_yn, NT)
            for k in range(KI):
                if k >= 4:
                    if k % 2:
                        pe.wait_ge(s_yta, (k - 4) // 2 + 1)
                    else:
                        pe.wait_ge(s_ytd, (k - 4) // 2 + 1)
                for t in range(NT):
                    ins = pe.transpose(ps[:, 4 + k % 4, t * P:(t + 1) * P], xs[:, t, k * P:(k + 1) * P], ident)
                ins.then_inc(s_yt, 1)
            pe.wait_ge(s_sz, 16)
            for m in range(KD):
                u = units["out"][m]
                arrived(pe, u)
                if m >= 4:
                    pe.wait_ge(s_h1, m - 3)
                w = slot(u, KI)
                for k in range(KI):
                    if m == 0:
                        if k % 2:
                            pe.wait_ge(s_yta, k // 2 + 1)
                        else:
                            pe.wait_ge(s_ytd, k // 2 + 1)
                    ins = pe.matmul(ps[:, m % 4, :], w[:, k, :], yT[:, k, :], start=(k == 0), stop=(k == KI - 1))
                ins.then_inc(s_op, 1)

            def moe_pe(l):
                n = TOK[l]
                nt = n // P
                for t in range(nt):
                    for k in range(KD):
                        if t == 0:
                            pe.wait_ge(s_a, KD * (2 * l + 1) + k + 1)
                        ins = pe.matmul(ps[:, 6, t * NE:(t + 1) * NE], aT[:, k, t * P:(t + 1) * P], rw[:, k, :],
                                        start=(k == 0), stop=(k == KD - 1))
                ins.then_inc(s_rl, 1)

                def expert(e):
                    first = isinstance(e, int)
                    w = [units[f"moe{l}"][j] for j in range(6)]
                    for f in range(KF):
                        q = KF * e + f
                        if f % 2 == 0:
                            arrived(pe, w[f], e)
                            arrived(pe, w[f + 1], e)
                        if not (first and q < 2):
                            pe.wait_ge(s_hid, GU0[l] + q - 1)
                        for r in range(2):
                            ws = slot(w[2 * (f // 2) + r])
                            for k in range(KD):
                                ins = pe.matmul(ps[:, 2 * (f % 2) + r, 0:n], ws[:, k, (f % 2) * P:(f % 2 + 1) * P],
                                                aT[:, k, 0:n], start=(k == 0), stop=(k == KD - 1))
                            if r == 1:
                                ins.then_inc(s_gu, 1)
                            elif f % 2 == 1:
                                ins.then_inc(s_gf, 1)
                    arrived(pe, w[4], e)
                    arrived(pe, w[5], e)
                    for r in range(NOUT[l]):
                        t, c = r // 2, r % 2
                        y = NOUT[l] * e + r
                        if first and y < 4:
                            pe.wait_ge(s_rs1, l + 1)
                        else:
                            pe.wait_ge(s_yu, Y0[l] + y - 3)
                        for k in range(KF):
                            if r == 0 and k % 3 == 0:
                                pe.wait_ge(s_hid, GU0[l] + KF * e + (3 if k == 0 else 4))
                            ins = pe.matmul(ps[:, 4 + r % 4, :], hid[:, k, t * P:(t + 1) * P],
                                            slot(w[4 + k // 2], 2)[:, k % 2, c * 512:(c + 1) * 512],
                                            start=(k == 0), stop=(k == KF - 1))
                            if r == NOUT[l] - 1 and k == 1:
                                ins.then_inc(s_y4, 1)
                        ins.then_inc(s_yn4, 1)

                expert(0)
                with pe.Fori(0, NE) as e:
                    expert(e + 1)
                pe.wait_ge(s_yu, Y0[l] + NOUT[l] * (NE + 1))
                for k in range(KD):
                    for t in range(nt):
                        ins = pe.transpose(ps[:, k, t * P:(t + 1) * P], acc[:, t, k * P:(k + 1) * P], ident)
                    ins.then_inc(s_mt, 1)

            pe.wait_ge(s_ytd, 8)
            pe.wait_ge(s_yta, 8)
            mean_square(1, T, 7)
            moe_pe(0)

            pe.wait_ge(s_h2, KD)
            mean_square(2, T, 7)
            pe.wait_ge(s_a, 3 * KD)
            for c in range(4):
                u = units["q"][c]
                arrived(pe, u)
                w = slot(u)
                for r in range(2):
                    for k in range(KD):
                        ins = pe.matmul(ps[:, c, r * S:(r + 1) * S], w[:, k, r * P:(r + 1) * P], aT[:, k, 0:S],
                                        start=(k == 0), stop=(k == KD - 1))
                ins.then_inc(s_q, 1)
            arrived(pe, units["k"][0])
            w = slot(units["k"][0])
            for m in range(2):
                for k in range(KD):
                    ins = pe.matmul(ps[:, 4 + m, :], w[:, k, m * P:(m + 1) * P], aT[:, k, :],
                                    start=(k == 0), stop=(k == KD - 1))
            ins.then_inc(s_kv, 1)
            arrived(pe, units["v"][0])
            pe.wait_ge(s_rs, 3)
            w = slot(units["v"][0])
            for t in range(NT):
                for k in range(KD):
                    ins = pe.matmul(ps[:, 6 + t // 2, (t % 2) * UC:(t % 2 + 1) * UC], aT[:, k, t * P:(t + 1) * P],
                                    w[:, k, :], start=(k == 0), stop=(k == KD - 1))
                if t % 2:
                    ins.then_inc(s_kv, 1)
            for c in range(4):
                pe.wait_ge(s_qc, c + 1)
                pe.matmul(ps[:, c, :], rope_m, QT[:, 2 * c:2 * c + 2, :], start=True, stop=True).then_inc(s_rot, 1)
            pe.wait_ge(s_kc, 2)
            pe.matmul(ps[:, 4, :].rearrange("p (c n) -> p c n", c=2), rope_m, KT[:, :, 0:S], start=True, stop=True)\
                .then_inc(s_rot, 1)
            pe.wait_ge(s_rp, 5)
            pe.wait_ge(s_kx, 32)
            pe.wait_ge(s_vv, 2)

            def scores(n):
                b, h = divmod(n, QH)
                kv = h // 4
                lo = slice((h % 2) * HD, (h % 2 + 1) * HD)
                keys = KT if kv % 2 == h % 2 else KX
                if n >= 2:
                    pe.wait_ge(s_p, n - 1)
                pe.matmul(ps[:, n % 2, :], identb, amask[b], start=True, stop=False)
                pe.matmul(ps[:, n % 2, :], QT[lo, h // 2, b * P:(b + 1) * P], keys[lo, kv // 2, :], start=False, stop=True)\
                    .then_inc(s_sc, 1)

            def turn_probs(n):
                pe.wait_ge(s_p, n + 1)
                if n >= 2:
                    pe.wait_ge(s_ptv, n - 1)
                for j in range(NT):
                    ins = pe.transpose(ps[:, 2 + n % 2, j * P:(j + 1) * P], pr[n % 2][:, j * P:(j + 1) * P], ident)
                ins.then_inc(s_pt, 1)

            def pv(n):
                b, h = divmod(n, QH)
                kv = h // 4
                pe.wait_ge(s_ptv, n + 1)
                for j in range(NT):
                    ins = pe.matmul(ps[:, 4 + 2 * b + h // 8, (h % 8) * HD:(h % 8 + 1) * HD], prT[n % 2][:, j * P:(j + 1) * P],
                                    V[:, j, kv * HD:(kv + 1) * HD], start=(j == 0), stop=(j == NT - 1))
                ins.then_inc(s_pv, 1)

            for n in range(34):
                if n < 32:
                    scores(n)
                if 1 <= n < 33:
                    turn_probs(n - 1)
                if n >= 2:
                    pv(n - 2)
            pe.wait_ge(s_o, 4)
            for k in range(8):
                for t in range(2):
                    ins = pe.transpose(ps[:, k // 2, (k % 2) * S + t * P:(k % 2) * S + (t + 1) * P],
                                       O[:, t, k * P:(k + 1) * P], ident)
                if k % 2:
                    ins.then_inc(s_ot, 1)
            for m in range(KD):
                u = units["ao"][m // 2]
                arrived(pe, u)
                if m >= 4:
                    pe.wait_ge(s_h1, KD + m - 3)
                w = slot(u)
                for k in range(8):
                    if m == 0 and k % 2 == 0:
                        pe.wait_ge(s_otv, k // 2 + 1)
                    ins = pe.matmul(ps[:, 4 + m % 4, 0:S], w[:, k, (m % 2) * P:(m % 2 + 1) * P], oT[:, k, :],
                                    start=(k == 0), stop=(k == 7))
                ins.then_inc(s_ao, 1)
            mean_square(3, S, 0)
            pe.wait_ge(s_h1, 2 * KD)
            pe.wait_ge(s_rs, 4)
            moe_pe(1)
            for t in range(2):
                for c in range(2):
                    pe.wait_ge(s_h2, 2 * KD)
                    for k in range(4):
                        ins = pe.transpose(ps[:, 2 * t + c, k * P:(k + 1) * P], hT[:, 4 * c + k, t * P:(t + 1) * P], ident)
                    ins.then_inc(s_ft, 1)

        @block.vector
        def _(dve):
            chain = [0]

            def link(ins):
                chain[0] += 1
                ins.then_inc(s_v, 1)
                dve.wait_ge(s_v, chain[0])

            dve.wait_ge(s_pkT, 1)
            dve.tensor_copy(par[:, :], ps[:, 0, 0:312]).then_inc(s_par, 1)
            for k in range(0, KD, 2):
                dve.wait_ge(s_xT, k + 1)
                dve.tensor_copy(hT[:, k, :], ps[:, (k + 1) % 8, :]).then_inc(s_hd, 1)

            def modulation(l, bank):
                dve.wait_ge(s_ada, ADA_U * (l + 1))
                dve.tensor_tensor(mod[:, l, :, :], ps[:, bank, 0:96].rearrange("p (j c) -> p j c", c=2),
                                  par[:, P + 48 * l:P + 48 * (l + 1)].unsqueeze(2).to_broadcast([P, 48, 2]), ALU.add)\
                    .then_inc(s_mod, 1)
                dve.wait_ge(s_mod, 3 * l + 1)
                for m in range(2):
                    w = par[:, P + 96 + 16 * m + KD * l:P + 96 + 16 * m + KD * (l + 1)]
                    dve.scalar_tensor_tensor(out=amod[:, l, m, :, :], in0=mod[:, l, 8 + 24 * m:16 + 24 * m, :], scalar=1.0,
                                             in1=w.unsqueeze(2).to_broadcast([P, KD, 2]), op0=ALU.add, op1=ALU.mult)\
                        .then_inc(s_mod, 1)

            def norm(i, n, bank):
                dve.wait_ge(s_ms, i + 1)
                link(dve.tensor_scalar(rstd[:, 0:n], ps[:, bank, 0:n], EPS, None, ALU.add))
                dve.reciprocal(rstd[:, 0:n], rstd[:, 0:n]).then_inc(s_rv, 1)
                dve.wait_ge(s_rs, i + 1)
                for k in range(KD):
                    dve.tensor_tensor(aT[:, k, 0:n], hT[:, k, 0:n], rstd[:, 0:n], ALU.mult).then_inc(s_nx, 1)

            norm(0, T, 7)
            modulation(0, 1)

            dve.wait_ge(s_bc, 16 * 7)
            dve.wait_ge(s_dt, 1)
            dve.tensor_tensor(sp[0].rearrange("p (t n) -> p t n", t=NT), ps[:, 5, 0:256].rearrange("p (t n) -> p t n", t=NT),
                              dtb[:, :].unsqueeze(1).to_broadcast([P, NT, 64]), ALU.add).then_inc(s_sp, 1)
            dve.wait_ge(s_sp, 1)
            link(dve.tensor_scalar(sp[7], sp[0], -1.0, None, ALU.mult))
            dve.tensor_tensor(sp[1], sp[0], sp[7], ALU.max).then_inc(s_sp, 1)
            dve.wait_ge(s_spe, 1)
            link(dve.tensor_scalar(sp[2], sp[1], 2.0, None, ALU.add))
            link(dve.reciprocal(sp[3], sp[2]))
            link(dve.tensor_tensor(sp[4], sp[1], sp[3], ALU.mult))
            link(dve.tensor_tensor(sp[5], sp[4], sp[4], ALU.mult))
            link(dve.tensor_scalar(sp[2], sp[5], 1.0 / 17, None, ALU.mult))
            for n in (15, 13, 11, 9, 7, 5, 3):
                link(dve.scalar_tensor_tensor(out=sp[2], in0=sp[2], scalar=1.0 / n, in1=sp[5], op0=ALU.add, op1=ALU.mult))
            link(dve.scalar_tensor_tensor(out=sp[2], in0=sp[2], scalar=1.0, in1=sp[4], op0=ALU.add, op1=ALU.mult))
            link(dve.tensor_scalar(sp[3], sp[0], 0.0, None, ALU.max))
            link(dve.scalar_tensor_tensor(out=dt[:, :, :].rearrange("p t n -> p (t n)"), in0=sp[2], scalar=2.0, in1=sp[3],
                                          op0=ALU.mult, op1=ALU.add))
            dve.wait_ge(s_spe, 2)
            dve.scalar_tensor_tensor(out=sp[6].rearrange("p (t n) -> p t n", t=NT), in0=dt[:, :, :], scalar=-1.0,
                                     in1=expa[:, :].unsqueeze(1).to_broadcast([P, NT, 64]), op0=ALU.mult, op1=ALU.mult)\
                .then_inc(s_dA, 1)

            def cum_copies():
                dve.wait_ge(s_cum, 1)
                dve.tensor_copy(cum[:, :, :].rearrange("p t n -> p (t n)"), ps[:, 6, 0:256]).then_inc(s_cumv, 1)
                dve.tensor_copy(cdec[:, :, :].rearrange("p t n -> p (t n)"), ps[:, 7, 0:256]).then_inc(s_cumv, 1)
                dve.wait_ge(s_cumv, 2)
                dve.tensor_tensor(wdt[:, :, :], cdec[:, :, :], cum[:, :, :], ALU.subtract).then_inc(s_cumv, 1)
                dve.tensor_scalar(ncum[:, :, :], cum[:, :, :], -1.0, None, ALU.mult).then_inc(s_cumv, 1)

            def conv(i):
                ch = i + KI if i < 8 else i - 8
                dve.wait_ge(s_pre, i + 1)
                if i >= 2:
                    dve.wait_ge(s_sil, i - 1)
                o = cacc[i % 2].rearrange("p (s n) -> p s n", s=2)
                link(dve.tensor_scalar(o, pre[i % 3][:, :, 0:S], par[:, ch:ch + 1], par[:, 272 + ch:273 + ch],
                                       ALU.mult, ALU.add))
                for tap in range(1, TAPS):
                    ins = dve.scalar_tensor_tensor(out=o, in0=pre[i % 3][:, :, tap:tap + S],
                                                   scalar=par[:, tap * NCONV + ch:tap * NCONV + ch + 1], in1=o,
                                                   op0=ALU.mult, op1=ALU.add)
                    if tap < TAPS - 1:
                        link(ins)
                ins.then_inc(s_conv, 1)

            for i in range(NCONV):
                conv(i)
                if i == 7:
                    cum_copies()
                if i == 12:
                    dve.wait_ge(s_cT, 1)
                    dve.tensor_copy(cumT[:, :], ps[0:64, 5, :]).then_inc(s_cTv, 1)
            modulation(1, 0)
            dve.wait_ge(s_exps, 3)
            dve.tensor_tensor(wdt[:, :, :], wdt[:, :, :], dt[:, :, :], ALU.mult).then_inc(s_wdt, 1)

            def heads(v, col):
                return v[:, col:col + HG].unsqueeze(2).to_broadcast([P, HG, HP])

            def per_head(v):
                return v.rearrange("p (h n) -> p h n", h=HG)

            def take_states(g):
                dve.wait_ge(s_b4, 7 * g + 1)
                dve.tensor_copy(cbs[g % 2], ps[:, 4, :]).then_inc(s_b4v, 1)
                for q, (d, t) in enumerate([(0, 2), (1, 3), (0, 3), (1, 2), (0, 0), (1, 1)]):
                    n = q // 2
                    if n == 0:
                        dve.wait_ge(s_b4, 7 * g + q + 2)
                        dve.tensor_copy(H[d][0], ps[:, 4, :]).then_inc(s_b4v, 1)
                    else:
                        dve.wait_ge(s_b4v, 7 * g + q)
                        link(dve.tensor_tensor(per_head(H[d][n]), per_head(H[d][n - 1]),
                                               heads(cdec[:, t, :], d * NH + g * HG), ALU.mult))
                        dve.wait_ge(s_b4, 7 * g + q + 2)
                        dve.tensor_tensor(H[d][n], H[d][n], ps[:, 4, :], ALU.add).then_inc(s_b4v, 1)

            for s in range(4 * NG):
                g, t = s // 4, TILE_ORDER[s % 4]
                cg = g * HG
                if s % 4 == 0:
                    take_states(g)
                for d in range(2):
                    dve.wait_ge(s_E, 4 * s + 2 * d + 2)
                    m = E[:, s % 2, d * HG:(d + 1) * HG, :]
                    if d == 0 and s % 4 == 0:
                        dve.wait_ge(s_b4v, 7 * g + 1)
                    dve.tensor_tensor(m, m, cbs[g % 2][:, t * P:(t + 1) * P].unsqueeze(1).to_broadcast([P, HG, P]),
                                      ALU.mult).then_inc(s_M, 1)
                dve.wait_ge(s_off, s + 1)
                if s >= 2:
                    dve.wait_ge(s_y, s - 1)
                y = yb[s % 2]
                if t == 2:
                    link(dve.tensor_tensor(per_head(y), per_head(ps[:, 7, :]), heads(ecum[:, t, :], NH + cg), ALU.mult))
                elif t == 3:
                    link(dve.tensor_tensor(per_head(y), per_head(ps[:, 6, :]), heads(ecum[:, t, :], cg), ALU.mult))
                else:
                    dve.tensor_tensor(per_head(y), per_head(ps[:, 6, :]), heads(ecum[:, t, :], cg), ALU.mult)
                    link(dve.tensor_tensor(per_head(rstd[:, :]), per_head(ps[:, 7, :]), heads(ecum[:, t, :], NH + cg),
                                           ALU.mult))
                    link(dve.tensor_tensor(y, y, rstd[:, :], ALU.add))
                dve.wait_ge(s_Y, s + 1)
                dve.tensor_tensor(y, y, ps[:, 5, :], ALU.add).then_inc(s_yo, 1)

            dve.wait_ge(s_y, 4 * NG)
            for b in range(16):
                t = 2 * (b % 2)
                dve.wait_ge(s_sz, b + 1)
                yv = xs[:, t:t + 2, (b // 2) * UC:(b // 2 + 1) * UC]
                dve.tensor_tensor(yv, yv, sz[b % 2].rearrange("p (t n) -> p t n", t=2), ALU.mult).then_inc(s_zy, 1)
            dve.wait_ge(s_ss, NT)
            link(dve.tensor_scalar(small[:, 12:16], small[:, 0:4], 1.0 / DI, EPS, ALU.mult, ALU.add))
            dve.reciprocal(small[:, 4:8], small[:, 12:16]).then_inc(s_ry, 1)
            dve.wait_ge(s_rq, 1)
            dve.wait_ge(s_zy, 16)
            for t in range(NT):
                dve.tensor_scalar(xs[:, t, :], xs[:, t, :], small[:, 8 + t:9 + t], None, ALU.mult).then_inc(s_yn, 1)
            for k in range(0, KI, 2):
                dve.wait_ge(s_yt, k + 1)
                dve.tensor_scalar(yT[:, k, :], ps[:, 4 + k % 4, :], par[:, 256 + k:257 + k], None, ALU.mult)\
                    .then_inc(s_ytd, 1)
            for m in range(KD):
                dve.wait_ge(s_op, m + 1)
                for q in range(2):
                    ins = dve.scalar_tensor_tensor(out=hT[:, m, q * S:(q + 1) * S], in0=ps[:, m % 4, q * S:(q + 1) * S],
                                                   scalar=mod[:, 0, 16 + m, q:q + 1], in1=hT[:, m, q * S:(q + 1) * S],
                                                   op0=ALU.mult, op1=ALU.add)
                ins.then_inc(s_h1, 1)

            def route(l):
                nt = TOK[l] // P
                n = nt * NE

                def v(i, m=n):
                    return rt[i][:, 0:m]

                def e3(i):
                    return rt[i][:, 0:n].rearrange("p (t e) -> p t e", e=NE)

                def g4(i):
                    return rt[i][:, 0:n].rearrange("p (g e) -> p g e", e=4)

                def tg(i):
                    return rt[i][:, 0:4 * nt].rearrange("p (t g) -> p t g", g=4)

                dve.wait_ge(s_rs1, l + 1)
                link(dve.tensor_tensor(e3(1), e3(0), rb[:, :].unsqueeze(1).to_broadcast([P, nt, NE]), ALU.add))
                b = g4(1)
                gs, pair = rt[2][:, 0:4 * nt], rt[3][:, 0:4 * nt]
                first = True
                for i in range(4):
                    for j in range(i + 1, 4):
                        o = gs if first else pair
                        link(dve.tensor_tensor(o.unsqueeze(2), b[:, :, i:i + 1], b[:, :, j:j + 1], ALU.add))
                        if not first:
                            link(dve.tensor_tensor(gs, gs, pair, ALU.max))
                        first = False
                best, eq = rt[4][:, 0:nt], tg(5)
                link(dve.tensor_reduce(best, tg(2), AX.X, ALU.max))
                link(dve.tensor_tensor(eq, tg(2), best.unsqueeze(2).to_broadcast([P, nt, 4]), ALU.is_equal))
                link(dve.tensor_tensor(eq, eq, erev[:, NE:NE + 4].unsqueeze(1).to_broadcast([P, nt, 4]), ALU.mult))
                link(dve.tensor_reduce(best, eq, AX.X, ALU.max))
                link(dve.tensor_tensor(eq, eq, best.unsqueeze(2).to_broadcast([P, nt, 4]), ALU.is_equal))
                gm = rt[5][:, 0:4 * nt].unsqueeze(2).to_broadcast([P, 4 * nt, 4])
                link(dve.tensor_tensor(g4(6), b, gm, ALU.mult))
                link(dve.tensor_scalar(rt[7][:, 0:4 * nt], rt[5][:, 0:4 * nt], -1.0, -NEG, ALU.add, ALU.mult))
                link(dve.tensor_tensor(g4(6), g4(6), rt[7][:, 0:4 * nt].unsqueeze(2).to_broadcast([P, 4 * nt, 4]), ALU.add))
                for i in range(2):
                    o = 8 + i
                    link(dve.tensor_reduce(best, e3(6), AX.X, ALU.max))
                    link(dve.tensor_tensor(e3(o), e3(6), best.unsqueeze(2).to_broadcast([P, nt, NE]), ALU.is_equal))
                    link(dve.tensor_tensor(e3(o), e3(o), erev[:, 0:NE].unsqueeze(1).to_broadcast([P, nt, NE]), ALU.mult))
                    link(dve.tensor_reduce(best, e3(o), AX.X, ALU.max))
                    link(dve.tensor_tensor(e3(o), e3(o), best.unsqueeze(2).to_broadcast([P, nt, NE]), ALU.is_equal))
                    if i == 0:
                        link(dve.scalar_tensor_tensor(out=v(6), in0=v(8), scalar=NEG, in1=v(6), op0=ALU.mult, op1=ALU.add))
                link(dve.tensor_tensor(v(8), v(8), v(9), ALU.add))
                link(dve.tensor_tensor(v(8), v(8), v(0), ALU.mult))
                link(dve.tensor_reduce(best, e3(8), AX.X, ALU.add))
                link(dve.reciprocal(rt[10][:, 0:nt], best))
                link(dve.tensor_tensor(comb[:, 0:nt, :], e3(8), rt[10][:, 0:nt].unsqueeze(2).to_broadcast([P, nt, NE]),
                                       ALU.mult))

            def moe_dve(l):
                n = TOK[l]

                def expert(e, w):
                    first = isinstance(e, int)
                    for f in range(KF):
                        q = KF * e + f
                        dve.wait_ge(s_sg, GU0[l] + q + 1)
                        dve.tensor_tensor(hid[:, f, 0:n], sg[f % 2][:, 0:n], ps[:, 2 * (f % 2) + 1, 0:n], ALU.mult)\
                            .then_inc(s_hid, 1)
                    for r in range(NOUT[l]):
                        t, c = r // 2, r % 2
                        y = NOUT[l] * e + r
                        dve.wait_ge(s_yn4, Y0[l] + y + 1)
                        o = acc[:, t, c * 512:(c + 1) * 512]
                        if first:
                            dve.tensor_copy(o, ps[:, 4 + r % 4, :]).then_inc(s_yu, 1)
                        else:
                            dve.wait_ge(s_yu, Y0[l] + y - NOUT[l] + 1)
                            dve.scalar_tensor_tensor(out=o, in0=ps[:, 4 + r % 4, :], scalar=w[:, t, :],
                                                     in1=o, op0=ALU.mult, op1=ALU.add).then_inc(s_yu, 1)

                route(l)
                expert(0, None)
                with dve.Fori(0, NE) as e:
                    expert(e + 1, comb[:, :, bass.ds(e, 1)])
                for k in range(KD):
                    dve.wait_ge(s_mt, KD * l + k + 1)
                    for q in range(n // S):
                        ins = dve.scalar_tensor_tensor(out=hT[:, k, q * S:(q + 1) * S], in0=ps[:, k, q * S:(q + 1) * S],
                                                       scalar=mod[:, l, 40 + k, q:q + 1], in1=hT[:, k, q * S:(q + 1) * S],
                                                       op0=ALU.mult, op1=ALU.add)
                    ins.then_inc(s_h2, 1)

            norm(1, T, 7)
            moe_dve(0)

            norm(2, T, 7)
            tabs = [v.unsqueeze(1).to_broadcast([P, 2, S]) for v in (cosT, sinT)]
            for c in range(5):
                x = QT[:, 2 * c:2 * c + 2, :] if c < 4 else KT[:, :, 0:S]
                rv = rq[c % 2].rearrange("p (c n) -> p c n", c=2)
                dve.wait_ge(s_rot, c + 1)
                if c >= 2:
                    dve.wait_ge(s_rp, c - 1)
                link(dve.tensor_tensor(rv, ps[:, c, :].rearrange("p (c n) -> p c n", c=2), tabs[1], ALU.mult))
                link(dve.tensor_tensor(x, x, tabs[0], ALU.mult))
                dve.tensor_tensor(x, x, rv, ALU.add).then_inc(s_rp, 1)
            for n in range(32):
                h = n % QH
                dve.wait_ge(s_sc, n + 1)
                dve.tensor_reduce(rmx[:, n:n + 1], ps[:, n % 2, :], AX.X, ALU.max).then_inc(s_mx, 1)
                dve.wait_ge(s_mx, 3 * n + 1)
                dve.tensor_scalar(mxa[:, n:n + 1], rmx[:, n:n + 1], SCALE, sink[:, h:h + 1], ALU.mult, ALU.max)\
                    .then_inc(s_mx, 1)
                dve.wait_ge(s_mx, 3 * n + 2)
                dve.tensor_scalar(nmx[:, n:n + 1], mxa[:, n:n + 1], -1.0, None, ALU.mult).then_inc(s_mx, 1)
            dve.tensor_tensor(esk.rearrange("p (b h) -> p b h", b=2), sink[:, :].unsqueeze(1).to_broadcast([P, 2, QH]),
                              mxa.rearrange("p (b h) -> p b h", b=2), ALU.subtract).then_inc(s_es0, 1)
            dve.wait_ge(s_esk, 1)
            link(dve.tensor_tensor(den, den, esk, ALU.add))
            link(dve.reciprocal(rden, den))
            dve.wait_ge(s_pv, 32)
            for n in range(4):
                b, c = n // 2, n % 2
                dve.tensor_tensor(O[:, b, c * 512:(c + 1) * 512].rearrange("p (h n) -> p h n", h=8),
                                  ps[:, 4 + n, :].rearrange("p (h n) -> p h n", h=8),
                                  rden[:, n * 8:(n + 1) * 8].unsqueeze(2).to_broadcast([P, 8, HD]), ALU.mult).then_inc(s_o, 1)
            for n in range(4):
                dve.wait_ge(s_ot, n + 1)
                dve.tensor_copy(oT[:, 2 * n:2 * n + 2, :], ps[:, n, :].rearrange("p (k n) -> p k n", k=2)).then_inc(s_otv, 1)
            for m in range(KD):
                dve.wait_ge(s_ao, m + 1)
                dve.scalar_tensor_tensor(out=hT[:, m, 0:S], in0=ps[:, 4 + m % 4, 0:S], scalar=mod[:, 1, 16 + m, 0:1],
                                         in1=hT[:, m, 0:S], op0=ALU.mult, op1=ALU.add).then_inc(s_h1, 1)
            norm(3, S, 0)
            moe_dve(1)

            for t in range(2):
                for c in range(2):
                    dve.wait_ge(s_ft, 2 * t + c + 1)
                    dve.tensor_copy(fin[:, t, c * 512:(c + 1) * 512], ps[:, 2 * t + c, :]).then_inc(s_fc, 1)
            dve.wait_ge(s_fs, 2)
            link(dve.tensor_scalar(small[:, 6:8], small[:, 0:2], 1.0 / D, EPS, ALU.mult, ALU.add))
            dve.reciprocal(small[:, 2:4], small[:, 6:8]).then_inc(s_fr, 1)
            dve.wait_ge(s_fq, 1)
            dve.wait_ge(s_fw, 16)
            for t in range(2):
                dve.scalar_tensor_tensor(out=fin[:, t, :], in0=fin[:, t, :], scalar=small[:, 4 + t:5 + t], in1=fnw,
                                         op0=ALU.mult, op1=ALU.mult).then_inc(s_fo, 1)


_INS = ["x", "c", "ctx", "c_ctx", "ada_w", "ada_b", "norm1_w", "norm2_w", "ssd_in_w", "ssd_conv_w", "ssd_conv_b",
        "ssd_dt_bias", "ssd_a_log", "ssd_d", "ssd_norm_w", "ssd_out_w", "attn_qkv_w", "attn_sink", "attn_out_w",
        "router_w", "router_bias", "moe_w_gate", "moe_w_up", "moe_w_down", "shared_w_gate", "shared_w_up",
        "shared_w_down", "final_norm_w"]


def kernel(**inputs):
    import concourse.bacc as bacc
    from concourse.bass_utils import run_bass_kernel_spmd

    nc = bacc.Bacc("TRN2", target_bir_lowering=False, num_devices=1)
    arrays = {n: np.ascontiguousarray(inputs[n]) for n in _INS}
    arrays["c32"], arrays["c16"], arrays["erev"] = host_constants()
    aps = {n: nc.dram_tensor(f"in_{n}", v.shape, mybir.dt.from_np(v.dtype), kind="ExternalInput").ap()
           for n, v in arrays.items()}
    out = nc.dram_tensor("out", (1, S, D), F32, kind="ExternalOutput").ap()
    build(nc, aps, out)
    r = run_bass_kernel_spmd(nc, [{f"in_{n}": v for n, v in arrays.items()}], core_ids=[0])
    return r.results[0]["out"]
```

```python
from contextlib import ExitStack

import numpy as np

import concourse.bass as bass
from concourse import mybir

F32 = mybir.dt.float32
BF16 = mybir.dt.bfloat16
U32 = mybir.dt.uint32
ALU = mybir.AluOpType
ACT = mybir.ActivationFunctionType
AX = mybir.AxisListType

P = 128
D = 1024
KD = D // P
S = 256
T = 2 * S
NT = T // P
EPS = 1e-6
DI = 2048
KI = DI // P
NH = 32
HP = 64
NG = 4
HG = NH // NG
GW = HG * HP
NCONV = (DI + 2 * NG * P) // P
TAPS = 5
PADS = (TAPS - 1) // 2
SEG = S + 2 * PADS
QH = 16
KVH = 4
HD = 64
SCALE = HD ** -0.5
WINDOW = 128
GRID_W = 64
NE = 16
FE = 512
CAP = [128, 96]
EMPTY = 8192
KF = FE // P
NEG = -1e30

SLOTS = 6
SLOT = 2048
UC = 256
ADA_U = 6 * D // UC

XBC0 = DI
TILE_ORDER = [2, 3, 0, 1]


def host_constants():
    k = np.arange(P)
    ident = np.eye(P, dtype=np.float32)
    tri_f = (k[:, None] <= k[None, :]).astype(np.float32)
    tri_b = (k[:, None] >= k[None, :]).astype(np.float32)
    rope_m = np.zeros((P, P), np.float32)
    pairs = HD // 4
    for m in range(P):
        base, half = m - (m % (2 * pairs)), (m // pairs) % 2
        p = m % pairs
        if half == 0:
            rope_m[base + pairs + p, m] = -1.0
        else:
            rope_m[base + p, m] = 1.0
    tok = np.arange(S)
    pos = np.stack([tok // GRID_W, tok % GRID_W], axis=0).astype(np.float32)
    inv = (np.float32(10000.0) ** (-np.arange(pairs, dtype=np.float32) / np.float32(pairs))).astype(np.float32)
    axis = (k % HD) // (2 * pairs)
    ang = (pos[axis] * inv[k % pairs][:, None]).astype(np.float32)
    c32 = np.concatenate([ident, tri_f, tri_b, rope_m, np.cos(ang), np.sin(ang)], axis=1).astype(np.float32)
    mask_f = np.where(k[None, :] >= k[:, None], 0.0, NEG)
    mask_b = np.where(k[None, :] <= k[:, None], 0.0, NEG)
    am = []
    for b in range(S // P):
        diff = np.abs(np.arange(S)[None, :] - (b * P + k)[:, None])
        am += [np.where(diff <= WINDOW, 0.0, NEG), np.zeros((P, S))]
    c16 = np.concatenate([ident, mask_f, mask_b] + am, axis=1).astype(np.float32)
    erev = np.tile(np.concatenate([np.arange(NE, 0, -1), np.arange(4, 0, -1), 1 + k]).astype(np.float32), (P, 1))
    val = np.zeros((P, NT, NE, 3), np.float32)
    val[..., 0] = k[:, None, None]
    val[..., 1] = 1 + np.arange(NT)[None, :, None]
    return c32, c16, erev, val.reshape(P, -1)


class Unit:

    def __init__(self, index, parts, arrived):
        self.index, self.parts, self.slot, self.arrived = index, parts, index % SLOTS, arrived


def plan_units(kinds):
    counts = [0] * SLOTS
    units, index = {}, 0
    for name, n, parts in kinds:
        units[name] = []
        for _ in range(n):
            counts[index % SLOTS] += 16 * parts
            units[name].append(Unit(index, parts, counts[index % SLOTS]))
            index += 1
    return units


def build(nc, a, out):
    units = plan_units([("ada0", ADA_U, 1), ("xbc", NCONV // 2, 1), ("ada1", ADA_U, 1), ("z", DI // UC, 1),
                        ("out", KD, 1), ("moe0", (NE + 1) * 6, 1), ("q", 4, 1), ("k", 1, 1), ("v", 1, 1),
                        ("ao", D // UC, 1), ("moe1", (NE + 1) * 6, 1)])
    order = [(n, v) for n in ("ada0", "xbc", "ada1", "z", "out") for v in range(len(units[n]))]
    order1 = [(n, v) for n in ("q", "k", "v", "ao") for v in range(len(units[n]))]

    with ExitStack() as ctx:
        def sb(name, shape, dt=F32):
            return ctx.enter_context(nc.sbuf_tensor(name, shape, dt))

        def sem(name):
            return ctx.enter_context(nc.semaphore(name))

        ring = sb("ring", [P, SLOTS, SLOT])
        hT = sb("hT", [P, KD, T])
        aT = sb("aT", [P, KD, T])
        big = sb("big", [P, 8192])
        ssb = sb("ssb", [P, 10240])
        tmp = sb("tmp", [P, 8192])
        c32 = sb("c32", [P, 4 * P + 2 * S])
        c16 = sb("c16", [P, 3 * P + 2 * T], BF16)
        erev = sb("erev", [P, NE + 4 + P])
        iota1 = erev[:, NE + 4:NE + 4 + P]
        wk = sb("wk", [P, 2, NT])
        gidx = sb("gidx", [P, NE], U32)
        sidx = sb("sidx", [P, NE], U32)
        flag = sb("flag", [1, 1], mybir.dt.int32)
        mark = sb("mark", [P, 2 * NE + 8])
        m_rows = nc.dram_tensor("m_rows", (T, D), F32, kind="Internal").ap()
        y_rows = [nc.dram_tensor(f"y_rows{l}", (2 * T, D), F32, kind="Internal").ap() for l in range(2)]
        ones = sb("ones", [P, P])
        mean = sb("mean", [P, P])
        par = sb("par", [P, 312])
        cs = sb("cs", [P, 2, KD])
        mod = sb("mod", [P, 2, 48, 2])
        amod = sb("amod", [P, 2, 2, KD, 2])
        rstd = sb("rstd", [P, T])
        rw = sb("rw", [P, KD, NE])
        rb = sb("rb", [P, NE])
        sink = sb("sink", [P, QH])
        comb = sb("comb", [P, NT, NE])
        dtb = sb("dtb", [P, 64])
        expa = sb("expa", [P, 64])
        dskip = sb("dskip", [P, NH])
        dt = sb("dt", [P, NT, 64])
        cum = sb("cum", [P, NT, 64])
        ncum = sb("ncum", [P, NT, 64])
        ecum = sb("ecum", [P, NT, 64])
        wdt = sb("wdt", [P, NT, 64])
        cdec = sb("cdec", [P, NT, 64])
        cumT = sb("cumT", [64, T])
        small = sb("small", [P, 16])
        ps = ctx.enter_context(nc.psum_tensor("ps", [P, 8, 512], F32))

        ident, tri_f, tri_b = c32[:, 0:P], c32[:, P:2 * P], c32[:, 2 * P:3 * P]
        rope_m, cosT, sinT = c32[:, 3 * P:4 * P], c32[:, 4 * P:4 * P + S], c32[:, 4 * P + S:4 * P + 2 * S]
        identb = c16[:, 0:P]
        dmask = [c16[:, P:2 * P], c16[:, 2 * P:3 * P]]
        amask = [c16[:, 3 * P + b * T:3 * P + (b + 1) * T] for b in range(2)]

        xtok = big[:, 0:4096].rearrange("p (t n) -> p t n", t=NT)
        xs = big[:, :].rearrange("p (t n) -> p t n", t=NT)
        BT = ssb[:, 0:2048].rearrange("p (g n) -> p g n", g=NG)
        CT = ssb[:, 2048:4096].rearrange("p (g n) -> p g n", g=NG)
        BK = ssb[:, 4096:6144].rearrange("p (t n) -> p t n", t=NT)
        E = ssb[:, 6144:10240].rearrange("p (b h i) -> p b h i", b=2, h=16)
        wdtw = ssb[:, 6144:6656].rearrange("p (k n) -> p k n", k=KD)
        sp = [ssb[:, 6656 + 256 * n:6912 + 256 * n] for n in range(8)]
        c16f = tmp[:, 4096:4096 + 3 * P + 2 * T]
        packs = tmp[:, 0:384].rearrange("p (i n) -> p i n", i=3)
        pre = [tmp[:, 520 * n:520 * n + 520].rearrange("p (s n) -> p s n", s=2) for n in range(3)]
        cacc = [tmp[:, 1560 + 512 * n:2072 + 512 * n] for n in range(2)]
        xsT = [tmp[:, 2584 + 512 * n:3096 + 512 * n] for n in range(2)]
        dtx = [[tmp[:, 1024 * b + 512 * d:1024 * b + 512 * d + 512] for d in range(2)] for b in range(2)]
        wx = [tmp[:, 2048 + 512 * n:2560 + 512 * n] for n in range(2)]
        H = [[tmp[:, 3072 + 512 * (3 * d + n):3584 + 512 * (3 * d + n)] for n in range(3)] for d in range(2)]
        yb = [tmp[:, 6144 + 512 * n:6656 + 512 * n] for n in range(2)]
        cbs = [tmp[:, 7168 + 512 * n:7680 + 512 * n] for n in range(2)]
        yT = ssb[:, 0:8192].rearrange("p (k n) -> p k n", k=KI)
        junk = ssb[:, 8192:10240]
        sz = [tmp[:, 512 * n:512 * n + 512] for n in range(2)]
        acc = big[:, 0:4096].rearrange("p (t n) -> p t n", t=NT)
        hid = big[:, 4096:6144].rearrange("p (k n) -> p k n", k=KF)
        sg = [big[:, 6144 + 512 * n:6656 + 512 * n] for n in range(2)]
        rt = [tmp[:, 64 * n:64 * n + 64] for n in range(16)]
        mtok = ssb[:, 0:4096].rearrange("p (t n) -> p t n", t=NT)
        Xg = ssb[:, 4096:5120]
        XgT = ssb[:, 5120:6144]
        Y = [ssb[:, 6144 + 1024 * n:7168 + 1024 * n] for n in range(2)]
        ypair = ssb[:, 0:8192].rearrange("p (t k n) -> p t k n", t=NT, k=2)
        onehot = tmp[:, 1024:5120].bitcast(BF16).rearrange("p (t e c) -> p t e c", t=NT, e=NE)
        val = tmp[:, 5120:5216].bitcast(BF16).rearrange("p (t e v) -> p t e v", t=NT, e=NE)
        valf = tmp[:, 5248:5440]
        rank = tmp[:, 5440:5504]
        slots = tmp[:, 5504:5552].rearrange("p (e v) -> p e v", e=NE)
        sl = [tmp[:, 5568 + 16 * n:5584 + 16 * n] for n in range(4)]
        QT = big[:, 0:2048].rearrange("p (c n) -> p c n", c=8)
        KT = big[:, 2048:3072].rearrange("p (c n) -> p c n", c=2)
        V = big[:, 3072:4096].rearrange("p (t n) -> p t n", t=NT)
        O = big[:, 4096:6144].rearrange("p (b n) -> p b n", b=2)
        oT = big[:, 6144:8192].rearrange("p (k n) -> p k n", k=8)
        rq = [ssb[:, 512 * n:512 * n + 512] for n in range(2)]
        pr = [ssb[:, 1024 + 512 * n:1536 + 512 * n] for n in range(2)]
        prT = [ssb[:, 2048 + 512 * n:2560 + 512 * n] for n in range(2)]
        KX = ssb[:, 5120:6144].rearrange("p (c n) -> p c n", c=2)
        rmx = ssb[:, 3072:3104]
        mxa = ssb[:, 3104:3136]
        nmx = ssb[:, 3136:3168]
        den = ssb[:, 3168:3200]
        esk = ssb[:, 3200:3232]
        rden = ssb[:, 3232:3264]
        fnw = ssb[:, 9216:10240]
        fin = ssb[:, 6144:8192].rearrange("p (t n) -> p t n", t=2)
        fsq = ssb[:, 8192:9216]

        n_consts, n_packs, n_x, n_bc = 3, 9, 2, 5
        s_const, s_pack, s_x, s_bc = sem("consts_in"), sem("packs_in"), sem("x_in"), sem("rows_in")
        s_set = sem("memsets")
        s_w = [sem(f"unit_in{n}") for n in range(SLOTS)]
        s_pkT, s_par = sem("packs_turned"), sem("params_ready")
        s_xT, s_hd, s_ha = sem("x_turned"), sem("hT_by_dve"), sem("hT_by_act")
        s_ada, s_mod = sem("ada_units"), sem("mod_ready")
        s_sq, s_ms, s_rs, s_nx, s_a = (sem("squares"), sem("mean_square"), sem("rstd_ready"),
                                             sem("normed"), sem("modulated"))
        s_ip, s_pre, s_conv, s_sil = sem("in_proj"), sem("conv_input"), sem("conv_done"), sem("conv_silu")
        s_tr, s_trev = sem("xbc_turned"), sem("xbc_tokens")
        s_dt, s_sp, s_cum, s_cumv, s_exps = (sem("dt_raw"), sem("softplus_steps"), sem("cum_ready"), sem("cum_copied"), sem("decays"))
        s_wdt, s_cT = sem("wdt_ready"), sem("cum_turned")
        s_v = sem("dve_chain")
        s_b4, s_b4v, s_wx = sem("cb_or_state"), sem("cb_or_state_taken"), sem("weighted_x")
        s_R, s_E, s_M, s_dtx = sem("cum_rows"), sem("decay_matrices"), sem("mixed_matrices"), sem("dt_x")
        s_off, s_Y, s_yo, s_pl, s_y = (sem("y_off"), sem("y_diag"), sem("y_summed"), sem("pool_chain"), sem("y_done"))
        s_z, s_sz, s_zy = sem("z_proj"), sem("silu_z"), sem("gated")
        s_ss, s_yn = sem("y_square_sum"), sem("y_normed")
        s_yt, s_ytd, s_yta = sem("y_turned"), sem("yT_by_dve"), sem("yT_by_act")
        s_op, s_h1 = sem("out_proj"), sem("h_plus_mixer")
        s_rl, s_rs1, s_cmb = sem("router_logits"), sem("router_sigmoid"), sem("combine_ready")
        s_gu, s_sg, s_hid, s_gf, s_y4, s_yn4, s_yu = (
            [sem(f"{n}{l}") for l in range(2)] for n in ("gate_up", "silu_gate", "hidden", "gate_unit", "down_unit",
                                                         "expert_out", "expert_out_used"))
        s_mt8, s_mtv, s_mr, s_val, s_sel, s_rk, s_oh, s_ix, s_flag, s_gi = (
            sem(n) for n in ("m_turned", "m_tokens", "m_rows_out", "val_in", "selection",
                                                         "ranks", "onehots", "slot_rows", "path_chosen", "slot_indices"))
        s_gx, s_xt, s_xa, s_xd, s_gu2, s_gf2, s_sg2, s_hid2 = (
            [sem(f"{n}{l}") for l in range(2)] for n in ("rows_gathered", "rows_turned", "rowsT_by_act",
                                                         "rowsT_by_dve", "gate_up_s", "gate_unit_s", "silu_s", "hidden_s"))
        s_y42, s_dn, s_ya, s_yd, s_scat, s_yf, s_acc = (
            [sem(f"{n}{l}") for l in range(2)] for n in ("down_unit_s", "down_s", "out_by_act", "out_by_dve",
                                                         "scattered", "out_buffers_free", "combined"))
        s_yp = [[sem(f"pairs_in{l}_{t}") for t in range(NT)] for l in range(2)]
        s_mt, s_h2 = sem("moe_turned"), sem("h_plus_moe")
        s_q, s_qc, s_rot, s_ro1, s_rp = (sem("q_units"), sem("qk_copied"), sem("rotated"), sem("rope_cos"),
                                         sem("rope_done"))
        s_kx = sem("keys_exchanged")
        s_kv, s_vv, s_kc = sem("kv_units"), sem("v_copied"), sem("k_copied")
        s_sc, s_mx, s_p, s_pt, s_ptv, s_pv = (sem("scores"), sem("row_max"), sem("probs"), sem("probs_turned"),
                                              sem("probsT"), sem("pv"))
        s_esk, s_o, s_ot, s_otv, s_ao = sem("sink_exp"), sem("o_ready"), sem("o_turned"), sem("oT_ready"), sem("attn_out")
        s_ft, s_fc, s_fs, s_fo, s_fw, s_fin = (sem("final_turned"), sem("final_copied"), sem("final_square"),
                                                     sem("final_ready"),
                                                     sem("final_w_in"), sem("out_written"))

        def hid_s(C):
            return big[:, 4096:4096 + KF * C].rearrange("p (k n) -> p k n", k=KF)

        NOUT = [2 * NT, NT]
        TOK = [T, S]

        def unit_free(name, v):
            return {"ada0": (s_ada, v + 1), "ada1": (s_ada, ADA_U + v + 1), "xbc": (s_ip, 2 * (v + 1)),
                    "z": (s_z, 2 * (v + 1)), "out": (s_op, v + 1), "q": (s_q, v + 1), "k": (s_kv, 1),
                    "v": (s_kv, 3), "ao": (s_ao, 2 * (v + 1))}[name]

        def expert_free(l, n, j):
            if j in (0, 2):
                return s_gf[l], 2 * n + 1 + j // 2
            if j in (1, 3):
                return s_gu[l], KF * n + j + 1
            if j == 4:
                return s_y4[l], n + 1
            return s_yn4[l], NOUT[l] * (n + 1)

        def sparse_free(l, e, j):
            if j in (0, 2):
                return s_gf2[l], 2 * e + 1 + j // 2
            if j in (1, 3):
                return s_gu2[l], 2 * e + 1 + j // 2
            if j == 4:
                return s_y42[l], e + 1
            return s_dn[l], 2 * (e + 1)

        def choose(eng, l):
            eng.wait_ge(s_flag, 1 * l + 1)
            return eng.value_load(flag[0:1, 0:1], min_val=0, max_val=1) == 0

        def cols(w, c0, width):
            return w[:, c0:c0 + width].rearrange("(k p) n -> p k n", p=P)

        def unit_source(name, v):
            if name in ("ada0", "ada1"):
                return cols(a["ada_w"][int(name[3])], v * UC, UC)
            if name == "xbc":
                c0 = XBC0 + DI + v * UC if v < 4 else XBC0 + (v - 4) * UC
                return cols(a["ssd_in_w"][0], c0, UC)
            if name == "z":
                return cols(a["ssd_in_w"][0], v * UC, UC)
            if name == "out":
                return cols(a["ssd_out_w"][0], v * P, P)
            if name == "q":
                return cols(a["attn_qkv_w"][0], v * UC, UC)
            if name == "k":
                return cols(a["attn_qkv_w"][0], QH * HD, UC)
            if name == "v":
                return cols(a["attn_qkv_w"][0], QH * HD + KVH * HD, UC)
            if name == "ao":
                return cols(a["attn_out_w"][0], v * UC, UC)

        def slot(u, k=KD):
            return ring[:, u.slot, :].rearrange("p (k n) -> p k n", k=k)

        def arrived(eng, u, n=0):
            eng.wait_ge(s_w[u.slot], u.arrived + n * 16)

        block = ctx.enter_context(nc.Block())

        @block.sync
        def _(sp_):
            sp_.dma_start(c32[:, :], a["c32"]).then_inc(s_const, 16)
            sp_.dma_start(c16f, a["c16"]).then_inc(s_const, 16)
            sp_.dma_start(erev[:, :], a["erev"]).then_inc(s_const, 16)
            packed = [(0, 0, a["ssd_conv_w"][0].rearrange("t (c p) -> (t c) p", p=P)),
                      (0, 120, a["final_norm_w"].rearrange("(c p) -> c p", p=P)),
                      (1, 0, a["ada_b"].rearrange("l (c p) -> (l c) p", p=P)),
                      (1, 96, a["norm1_w"].rearrange("l (c p) -> (l c) p", p=P)),
                      (1, 112, a["norm2_w"].rearrange("l (c p) -> (l c) p", p=P)),
                      (2, 0, a["ssd_norm_w"].rearrange("l (c p) -> (l c) p", p=P)),
                      (2, 16, a["ssd_conv_b"].rearrange("l (c p) -> (l c) p", p=P)),
                      (2, 40, a["c"].rearrange("l (c p) -> (l c) p", p=P)),
                      (2, 48, a["c_ctx"].rearrange("(c p) -> c p", p=P))]
            for i, r, src in packed:
                sp_.dma_start(packs[r:r + src.shape[0], i, :], src).then_inc(s_pack, 16)
            sp_.dma_start(xtok[:, 0:2, :], a["x"][0].rearrange("(t p) n -> p t n", p=P)).then_inc(s_x, 16)
            sp_.dma_start(xtok[:, 2:4, :], a["ctx"][0].rearrange("(t p) n -> p t n", p=P)).then_inc(s_x, 16)

            events = []

            def load(name, v):
                u = units[name][v]
                if u.index >= SLOTS:
                    s, n = events[u.index - SLOTS]
                    sp_.wait_ge(s, n)
                sp_.dma_start(slot(u, KI if name == "out" else KD), unit_source(name, v)).then_inc(s_w[u.slot], 16)
                events.append(unit_free(name, v))

            def expert_units(l, free, n, gate, up, down):
                for j in range(6):
                    u = units[f"moe{l}"][j]
                    sp_.wait_ge(*free(j))
                    h = j // 2
                    if j < 4:
                        src = (gate, up)[j % 2][:, h * UC:(h + 1) * UC].rearrange("(k p) n -> p k n", p=P)
                        dst = slot(u)
                    else:
                        src = down[(j - 4) * 2 * P:(j - 3) * 2 * P, :].rearrange("(k p) n -> p k n", p=P)
                        dst = slot(u, 2)
                    sp_.dma_start(dst, src).then_inc(s_w[u.slot], 16)

            def routed(l, free, e):
                w = [a[n][l, e if isinstance(e, slice) else bass.ds(e, 1)].rearrange("o k n -> (o k) n")
                     for n in ("moe_w_gate", "moe_w_up", "moe_w_down")]
                expert_units(l, free, e, *w)

            def moe(l):
                first = units[f"moe{l}"][0].index
                expert_units(l, lambda j: events[first + j - SLOTS], 0,
                             a["shared_w_gate"][l], a["shared_w_up"][l], a["shared_w_down"][l])
                sparse = choose(sp_, l)
                with sp_.If(sparse):
                    routed(l, lambda j: expert_free(l, 0, j), slice(0, 1))
                    routed(l, lambda j: sparse_free(l, 0, j), slice(1, 2))
                    with sp_.Fori(2, NE) as e:
                        routed(l, lambda j: sparse_free(l, e - 1, j), e)
                with sp_.Else():
                    with sp_.Fori(0, NE) as e:
                        routed(l, lambda j: expert_free(l, e, j), e)
                events.extend([(s_mt, KD * l + 1)] * (6 * (NE + 1)))

            for name, v in order:
                load(name, v)
            moe(0)
            for name, v in order1:
                load(name, v)
            moe(1)
            for t in range(2):
                sp_.wait_ge(s_fo, t + 1)
                sp_.dma_start(out[0, t * P:(t + 1) * P, :], fin[:, t, :]).then_inc(s_fin, 16)
            sp_.wait_ge(s_fin, 32)

        @block.gpsimd
        def _(pool):
            pool.memset(ones[:, :], 1.0).then_inc(s_set, 1)
            pool.memset(mean[:, :], 1.0 / D).then_inc(s_set, 1)
            pool.wait_ge(s_const, 16 * n_consts)
            pool.tensor_copy(c16[:, :], c16f).then_inc(s_set, 1)
            pool.memset(mark[:, 7:8], 0.0).then_inc(s_set, 1)
            pool.wait_ge(s_pkT, 1)
            for n in range(3):
                pool.memset(pre[n][:, :, 0:PADS], 0.0).then_inc(s_set, 1)
                pool.memset(pre[n][:, :, PADS + S:SEG], 0.0).then_inc(s_set, 1)

            def heads(v, col):
                return v[:, col:col + HG].unsqueeze(2).to_broadcast([P, HG, HP])

            def per_head(v):
                return v.rearrange("p (h n) -> p h n", h=HG)

            pool.wait_ge(s_trev, 20)
            pool.wait_ge(s_wdt, 1)
            for g in range(NG):
                cg = slice(g * GW, (g + 1) * GW)
                for q, (d, t) in enumerate([(0, 2), (1, 3), (0, 3), (1, 2), (0, 0), (1, 1)]):
                    n = 6 * g + q
                    if n >= 2:
                        pool.wait_ge(s_b4, 7 * ((n - 2) // 6) + (n - 2) % 6 + 2)
                    pool.tensor_tensor(per_head(wx[n % 2]), per_head(xs[:, t, cg]), heads(wdt[:, t, :], d * NH + g * HG),
                                       ALU.mult).then_inc(s_wx, 1)
                for i, t in enumerate(TILE_ORDER):
                    s = 4 * g + i
                    if s >= 2:
                        pool.wait_ge(s_Y, s - 1)
                    for d in range(2):
                        pool.tensor_tensor(per_head(dtx[s % 2][d]), per_head(xs[:, t, cg]),
                                           heads(dt[:, t, :], d * NH + g * HG), ALU.mult).then_inc(s_dtx, 1)
                    pool.wait_ge(s_dtx, 2 * s + 2)
                    pool.tensor_tensor(per_head(xs[:, t, cg]), per_head(xs[:, t, cg]), heads(dskip[:, :], g * HG),
                                       ALU.mult).then_inc(s_pl, 1)
                    pool.wait_ge(s_pl, s + 1)
                    pool.wait_ge(s_yo, s + 1)
                    pool.tensor_tensor(xs[:, t, cg], xs[:, t, cg], yb[s % 2], ALU.add).then_inc(s_y, 1)

            def moe_pool(l):
                C = CAP[l]
                pool.wait_ge(s_a, KD * (2 * l + 2))
                pool.wait_ge(s_val, 18 * l + 16)
                pool.tensor_copy(val[:, :, :, :].rearrange("p t e v -> p (t e v)"), valf).then_inc(s_val, 1)
                pool.memset(Xg, 0.0).then_inc(s_yf[l], 1)
                pool.memset(mark[:, 8 + NE * l:9 + NE * l], 0.0).then_inc(s_yf[l], 1)
                sparse = choose(pool, l)
                with pool.If(sparse):
                    pool.wait_ge(s_gi, 3 * l + 3)
                    pool.wait_ge(s_mr, 16 * l + 16)
                    pool.wait_ge(s_yf[l], 2)

                    def gather(e):
                        pool.indirect_dma_start(Xg[0:C, :], None, m_rows,
                                                bass.IndirectOffsetOnAxis(gidx[0:C, e:e + 1], 0),
                                                bounds_check=T - 1, oob_is_err=False).then_inc(s_gx[l], 16)

                    gather(0)
                    for e in range(NE):
                        pool.wait_ge(s_xt[l], e + 1)
                        gather((e + 1) % NE)
                        if e:
                            pool.wait_ge(s_scat[l], 16 * e)
                            pool.memset(mark[:, 8 + NE * l + e:9 + NE * l + e], 0.0).then_inc(s_yf[l], 1)
                        pool.wait_ge(s_ya[l], e + 2)
                        pool.wait_ge(s_yd[l], e + 2)
                        pool.indirect_dma_start(y_rows[l], bass.IndirectOffsetOnAxis(sidx[0:C, e:e + 1], 0),
                                                Y[e % 2][0:C, :], None, bounds_check=2 * T - 1, oob_is_err=False)\
                            .then_inc(s_scat[l], 16)

            moe_pool(0)
            moe_pool(1)

        @block.scalar
        def _(act):
            act.dma_start(wdtw, a["ssd_in_w"][0][:, DI + NCONV * P:DI + NCONV * P + 64].rearrange("(k p) n -> p k n", p=P))\
                .then_inc(s_bc, 16)
            act.dma_start(rw[:, :, :], a["router_w"].rearrange("(k p) n -> p k n", p=P)).then_inc(s_bc, 16)
            rows = [(dtb[:, :], a["ssd_dt_bias"].rearrange("l d h -> (l d h)")),
                    (expa[:, :], a["ssd_a_log"].rearrange("l d h -> (l d h)")),
                    (dskip[:, :], a["ssd_d"].rearrange("l h -> (l h)")),
                    (rb[:, :], a["router_bias"]), (sink[:, :], a["attn_sink"].rearrange("l h -> (l h)"))]
            for dst, src in rows:
                act.dma_start(dst, src.partition_broadcast(P)).then_inc(s_bc, 16)

            act.wait_ge(s_par, 1)
            act.activation(cs[:, :, :], par[:, 296:312].rearrange("p (c k) -> p c k", c=2), ACT.Silu).then_inc(s_par, 1)
            for k in range(1, KD, 2):
                act.wait_ge(s_xT, k + 1)
                act.copy(hT[:, k, :], ps[:, (k + 1) % 8, :]).then_inc(s_ha, 1)

            def norm_modulate(l, m, n, ready):
                i = 2 * l + m
                for k in range(KD):
                    ready(k)
                    act.activation(aT[:, k, 0:n], hT[:, k, 0:n], ACT.Square).then_inc(s_sq, 1)
                act.wait_ge(s_rs, 2 * i + 1)
                act.activation(rstd[:, 0:n], rstd[:, 0:n], ACT.Sqrt).then_inc(s_rs, 1)
                if i == 0:
                    act.wait_ge(s_mod, 3)
                elif l == 1 and m == 0:
                    act.wait_ge(s_mod, 6)
                for k in range(KD):
                    act.wait_ge(s_nx, KD * i + k + 1)
                    for q in range(n // S):
                        ins = act.activation(aT[:, k, q * S:(q + 1) * S], aT[:, k, q * S:(q + 1) * S], ACT.Identity,
                                             bias=mod[:, l, 24 * m + k, q:q + 1], scale=amod[:, l, m, k, q:q + 1])
                    ins.then_inc(s_a, 1)

            def ready0(k):
                if k % 2:
                    act.wait_ge(s_ha, k // 2 + 1)
                else:
                    act.wait_ge(s_hd, k // 2 + 1)

            norm_modulate(0, 0, T, ready0)

            act.wait_ge(s_sp, 2)
            act.activation(sp[1], sp[1], ACT.Exp, scale=-1.0).then_inc(s_sp, 1)
            act.wait_ge(s_bc, 16 * 7)
            act.activation(expa[:, :], expa[:, :], ACT.Exp).then_inc(s_sp, 1)

            def decays():
                act.wait_ge(s_cumv, 4)
                act.activation(ecum[:, :, :], cum[:, :, :], ACT.Exp).then_inc(s_exps, 1)
                act.activation(cdec[:, :, :], cdec[:, :, :], ACT.Exp).then_inc(s_exps, 1)
                act.activation(wdt[:, :, :], wdt[:, :, :], ACT.Exp).then_inc(s_exps, 1)

            def conv_in(i):
                act.wait_ge(s_ip, i + 1)
                if i >= 3:
                    act.wait_ge(s_conv, i - 2)
                else:
                    act.wait_ge(s_set, 10)
                act.copy(pre[i % 3][:, :, PADS:PADS + S], ps[:, i % 3, :].rearrange("p (s n) -> p s n", s=2))\
                    .then_inc(s_pre, 1)

            def conv_silu(i):
                act.wait_ge(s_conv, i + 1)
                if i < 4:
                    dst = BT[:, i, :]
                elif i < 8:
                    dst = CT[:, i - 4, :]
                else:
                    dst = xsT[i % 2]
                    if i >= 10:
                        act.wait_ge(s_tr, i - 5)
                act.activation(dst, cacc[i % 2], ACT.Silu).then_inc(s_sil, 1)

            def tokens(i):
                if 4 <= i < 8:
                    return
                j = i if i < 4 else i - 4
                act.wait_ge(s_tr, j + 1)
                src = ps[:, 3 + j % 2, :].rearrange("p (t n) -> p t n", t=NT)
                dst = BK[:, :, i * P:(i + 1) * P] if i < 4 else xs[:, :, (i - 8) * P:(i - 7) * P]
                act.copy(dst, src).then_inc(s_trev, 1)

            for i in range(NCONV + 3):
                if i < NCONV:
                    conv_in(i)
                if 0 <= i - 1 < NCONV:
                    conv_silu(i - 1)
                if 0 <= i - 3 < NCONV:
                    tokens(i - 3)
            decays()

            for s in range(4 * NG):
                g, t = s // 4, TILE_ORDER[s % 4]
                if s >= 2:
                    act.wait_ge(s_Y, s - 1)
                for q in range(4):
                    act.wait_ge(s_R, 4 * s + q + 1)
                    for j in range(4):
                        h = 4 * q + j
                        col = (h // HG) * NH + g * HG + h % HG
                        ins = act.activation(E[:, s % 2, h, :], ps[:, q, j * P:(j + 1) * P], ACT.Exp,
                                             bias=ncum[:, t, col:col + 1])
                    ins.then_inc(s_E, 1)

            for b in range(16):
                act.wait_ge(s_z, b + 1)
                if b >= 2:
                    act.wait_ge(s_zy, b - 1)
                act.activation(sz[b % 2], ps[:, b % 4, :], ACT.Silu).then_inc(s_sz, 1)
            act.wait_ge(s_zy, 16)
            for t in range(NT):
                act.activation(junk, xs[:, t, :], ACT.Square, accum_out=small[:, t:t + 1]).then_inc(s_ss, 1)
                act.wait_ge(s_ss, t + 1)
            act.wait_ge(s_ss, NT + 1)
            act.activation(small[:, 8:12], small[:, 4:8], ACT.Sqrt).then_inc(s_ss, 1)
            for k in range(1, KI, 2):
                act.wait_ge(s_yt, k + 1)
                act.activation(yT[:, k, :], ps[:, 4 + k % 4, :], ACT.Copy, scale=par[:, 256 + k:257 + k]).then_inc(s_yta, 1)

            def moe_act(l):
                n = TOK[l]
                nt = n // P
                C = CAP[l]

                def chunk(e, f):
                    q = KF * e + f
                    act.wait_ge(s_gu[l], q + 1)
                    if not (isinstance(e, int) and q < 2):
                        act.wait_ge(s_hid[l], q - 1)
                    act.activation(sg[f % 2][:, 0:n], ps[:, 2 * (f % 2), 0:n], ACT.Silu).then_inc(s_sg[l], 1)

                act.dma_start(valf, a["val"]).then_inc(s_val, 16)
                act.wait_ge(s_rl, l + 1)
                act.activation(rt[0][:, 0:nt * NE], ps[:, 6, 0:nt * NE], ACT.Sigmoid).then_inc(s_rs1, 1)
                chunk(0, 0)
                for r in range(2 * nt):
                    act.wait_ge(s_mt8, 8 * l + r + 1)
                    act.copy(mtok[:, r // 2, (r % 2) * 512:(r % 2 + 1) * 512], ps[:, (4, 7)[r % 2], :]).then_inc(s_mtv, 1)
                act.wait_ge(s_mtv, 8 * l + 2 * nt)
                act.dma_start(m_rows[0:n, :].rearrange("(t p) n -> p t n", p=P), mtok[:, 0:nt, :]).then_inc(s_mr, 16)
                for f in range(1, KF):
                    chunk(0, f)
                act.copy(mark[:, l:l + 1], ones[:, 0:1]).then_inc(s_ya[l], 1)
                sparse = choose(act, l)
                with act.If(sparse):
                    act.wait_ge(s_xt[l], 1)
                    act.copy(XgT[:, 0:4 * C], ps[:, 6, 0:4 * C]).then_inc(s_xa[l], 1)
                    with act.Fori(0, NE, 2) as e2:
                        for b in range(2):
                            e = e2 + b
                            for p in range(2):
                                act.wait_ge(s_gu2[l], 2 * e + p + 1)
                                act.activation(sg[p][:, 0:2 * C], ps[:, 2 * p, 0:2 * C], ACT.Silu).then_inc(s_sg2[l], 1)
                            act.wait_ge(s_xt[l], e + 2)
                            act.copy(XgT[:, 0:4 * C], ps[:, 6, 0:4 * C]).then_inc(s_xa[l], 1)
                            act.wait_ge(s_dn[l], 2 * e + 1)
                            act.wait_ge(s_yf[l], e + 1)
                            act.copy(Y[b][0:C, 0:512], ps[0:C, 4, :]).then_inc(s_ya[l], 1)
                    act.wait_ge(s_scat[l], 16 * NE)
                    act.wait_ge(s_xt[l], NE + 1)
                    act.wait_ge(s_dn[l], 2 * NE)
                    act.wait_ge(s_xd[l], NE + 1)
                    act.wait_ge(s_xa[l], NE + 1)
                    pairs = y_rows[l].rearrange("(k t p) n -> p t k n", k=2, p=P)
                    for t in range(nt):
                        act.dma_start(ypair[:, t, :, :], pairs[:, t, :, :]).then_inc(s_yp[l][t], 16)
                with act.Else():
                    with act.Fori(0, NE) as e:
                        for f in range(KF):
                            chunk(e + 1, f)

            norm_modulate(0, 1, T, lambda k: act.wait_ge(s_h1, k + 1))
            moe_act(0)

            norm_modulate(1, 0, T, lambda k: act.wait_ge(s_h2, k + 1))
            for c in range(4):
                act.wait_ge(s_q, c + 1)
                act.copy(QT[:, 2 * c:2 * c + 2, :], ps[:, c, :].rearrange("p (c n) -> p c n", c=2)).then_inc(s_qc, 1)
            act.wait_ge(s_kv, 1)
            for m in range(2):
                act.copy(KT[:, m, :], ps[:, 4 + m, :]).then_inc(s_kc, 1)
            for c in range(2):
                act.wait_ge(s_kv, 2 + c)
                act.copy(V[:, 2 * c:2 * c + 2, :], ps[:, 6 + c, :].rearrange("p (c n) -> p c n", c=2)).then_inc(s_vv, 1)

            act.wait_ge(s_rp, 5)
            for w in range(2):
                act.dma_start(KX[(1 - w) * HD:(2 - w) * HD, :, :], KT[w * HD:(w + 1) * HD, :, :]).then_inc(s_kx, 16)

            def probs(n):
                act.wait_ge(s_mx, 3 * n + 3)
                if n >= 2:
                    act.wait_ge(s_pt, n - 1)
                act.activation(pr[n % 2], ps[:, n % 2, :], ACT.Exp, bias=nmx[:, n:n + 1], scale=SCALE,
                               accum_out=den[:, n:n + 1]).then_inc(s_p, 1)

            def turned(n):
                act.wait_ge(s_pt, n + 1)
                if n >= 2:
                    act.wait_ge(s_pv, n - 1)
                act.copy(prT[n % 2], ps[:, 2 + n % 2, :]).then_inc(s_ptv, 1)

            for n in range(33):
                if n < 32:
                    probs(n)
                if n >= 1:
                    turned(n - 1)
            act.wait_ge(s_esk, 1)
            act.activation(esk, esk, ACT.Exp).then_inc(s_esk, 1)
            act.dma_start(fnw, a["final_norm_w"].partition_broadcast(P)).then_inc(s_fw, 16)
            norm_modulate(1, 1, S, lambda k: act.wait_ge(s_h1, KD + k + 1))
            moe_act(1)

            for t in range(2):
                act.wait_ge(s_fc, 2 * (t + 1))
                if t:
                    act.wait_ge(s_fs, 1)
                act.activation(fsq, fin[:, t, :], ACT.Square, accum_out=small[:, t:t + 1]).then_inc(s_fs, 1)
            act.wait_ge(s_fs, 3)
            act.activation(small[:, 4:6], small[:, 2:4], ACT.Sqrt).then_inc(s_fs, 1)

        @block.tensor
        def _(pe):
            pe.wait_ge(s_const, 16 * n_consts)
            pe.wait_ge(s_pack, 16 * n_packs)
            for i, rows in enumerate((P, P, 56)):
                ins = pe.transpose(ps[:, 0, i * P:i * P + rows], packs[0:rows, i, :], ident[0:rows, 0:rows])
            ins.then_inc(s_pkT, 1)
            pe.wait_ge(s_x, 32)
            for k in range(KD):
                if k == 7:
                    pe.wait_ge(s_par, 1)
                for t in range(NT):
                    ins = pe.transpose(ps[:, (k + 1) % 8, t * P:(t + 1) * P], xtok[:, t, k * P:(k + 1) * P], ident)
                ins.then_inc(s_xT, 1)

            def ada(l, bank):
                for v, u in enumerate(units[f"ada{l}"]):
                    arrived(pe, u)
                    w = slot(u)
                    for c in range(2):
                        j = 2 * (2 * v + c)
                        for k in range(KD):
                            ins = pe.matmul(ps[:, bank, j:j + 2], w[:, k, c * P:(c + 1) * P], cs[:, :, k],
                                            start=(k == 0), stop=(k == KD - 1))
                    ins.then_inc(s_ada, 1)

            def mean_square(i, n, bank):
                for k in range(KD):
                    pe.wait_ge(s_sq, KD * i + k + 1)
                    ins = pe.matmul(ps[:, bank, 0:n], mean[:, :], aT[:, k, 0:n], start=(k == 0), stop=(k == KD - 1))
                ins.then_inc(s_ms, 1)

            pe.wait_ge(s_set, 2)
            pe.wait_ge(s_hd, 4)
            pe.wait_ge(s_ha, 4)
            mean_square(0, T, 7)
            pe.wait_ge(s_par, 2)
            ada(0, 1)

            pe.wait_ge(s_bc, 16 * 7)
            pe.wait_ge(s_a, KD)
            for t in range(NT):
                for k in range(KD):
                    ins = pe.matmul(ps[:, 5, t * 64:(t + 1) * 64], aT[:, k, t * P:(t + 1) * P], wdtw[:, k, :],
                                    start=(k == 0), stop=(k == KD - 1))
            ins.then_inc(s_dt, 1)

            def turn_chunk(i):
                if 4 <= i < 8:
                    return
                j = i if i < 4 else i - 4
                pe.wait_ge(s_sil, i + 1)
                if j >= 2:
                    pe.wait_ge(s_trev, j - 1)
                src = BT[:, i, :] if i < 4 else xsT[i % 2]
                for t in range(NT):
                    ins = pe.transpose(ps[:, 3 + j % 2, t * P:(t + 1) * P], src[:, t * P:(t + 1) * P], ident)
                ins.then_inc(s_tr, 1)

            for i in range(NCONV + 2):
                if i < NCONV:
                    u = units["xbc"][i // 2]
                    arrived(pe, u)
                    if i == 1:
                        pe.wait_ge(s_mod, 1)
                    if i >= 3:
                        pe.wait_ge(s_pre, i - 2)
                    w = slot(u)
                    for k in range(KD):
                        ins = pe.matmul(ps[:, i % 3, :], w[:, k, (i % 2) * P:(i % 2 + 1) * P], aT[:, k, :],
                                        start=(k == 0), stop=(k == KD - 1))
                    ins.then_inc(s_ip, 1)
                if i >= 2:
                    turn_chunk(i - 2)
                if i == 6:
                    pe.wait_ge(s_sp, 5)
                    for t in range(NT):
                        pe.matmul(ps[:, 6, t * 64:t * 64 + 32], tri_f, sp[6][:, t * 64:t * 64 + 32], start=True, stop=True)
                        pe.matmul(ps[:, 6, t * 64 + 32:t * 64 + 64], tri_b, sp[6][:, t * 64 + 32:t * 64 + 64],
                                  start=True, stop=True)
                    pe.matmul(ps[:, 7, 0:256], ones[:, :], sp[6], start=True, stop=True).then_inc(s_cum, 1)
                if i == 10:
                    pe.wait_ge(s_cumv, 1)
                    for t in range(NT):
                        ins = pe.transpose(ps[0:64, 5, t * P:(t + 1) * P], cum[:, t, :], ident)
                    ins.then_inc(s_cT, 1)

            pe.wait_ge(s_pre, NCONV)
            ada(1, 0)

            def cb(g):
                if g:
                    pe.wait_ge(s_b4v, 7 * g)
                else:
                    pe.wait_ge(s_trev, 20)
                for t in range(NT):
                    ins = pe.matmul(ps[:, 4, t * P:(t + 1) * P], BT[:, g, t * P:(t + 1) * P],
                                    CT[:, g, t * P:(t + 1) * P], start=True, stop=True)
                ins.then_inc(s_b4, 1)

            def states(g):
                for q, (d, t) in enumerate([(0, 2), (1, 3), (0, 3), (1, 2), (0, 0), (1, 1)]):
                    pe.wait_ge(s_b4v, 7 * g + q + 1)
                    pe.wait_ge(s_wx, 6 * g + q + 1)
                    pe.matmul(ps[:, 4, :], BK[:, t, g * P:(g + 1) * P], wx[q % 2], start=True, stop=True).then_inc(s_b4, 1)

            def cum_rows(s):
                g, t = s // 4, TILE_ORDER[s % 4]
                for q in range(4):
                    if s:
                        pe.wait_ge(s_E, 4 * (s - 1) + q + 1)
                    d = q // 2
                    bank = ps[:, q, :].rearrange("p (h i) -> p h i", h=4)
                    pe.matmul(bank, identb, dmask[d].unsqueeze(1).to_broadcast([P, 4, P]), start=True, stop=False,
                              skip_group_check=True)
                    for j in range(4):
                        h = 4 * q + j
                        col = d * NH + g * HG + h % HG
                        ins = pe.matmul(bank[:, j, :], ident[0:64, col:col + 1].to_broadcast([64, P]),
                                        cumT[:, t * P:(t + 1) * P], start=False, stop=(j == 3), skip_group_check=True)
                    ins.then_inc(s_R, 1)

            def y_off(s):
                g, t = s // 4, TILE_ORDER[s % 4]
                if s:
                    pe.wait_ge(s_yo, s)
                pe.wait_ge(s_b4v, 7 * g + 7)
                lhs = CT[:, g, t * P:(t + 1) * P]
                if t != 2:
                    ins = pe.matmul(ps[:, 6, :], lhs, H[0][{3: 0, 0: 1, 1: 2}[t]], start=True, stop=True)
                if t != 3:
                    ins = pe.matmul(ps[:, 7, :], lhs, H[1][{2: 0, 1: 1, 0: 2}[t]], start=True, stop=True)
                ins.then_inc(s_off, 1)

            def y_diag(s):
                pe.wait_ge(s_dtx, 2 * s + 2)
                pe.wait_ge(s_M, 2 * s + 2)
                for h in range(HG):
                    for d in range(2):
                        ins = pe.matmul(ps[:, 5, h * HP:(h + 1) * HP], E[:, s % 2, d * HG + h, :],
                                        dtx[s % 2][d][:, h * HP:(h + 1) * HP], start=(d == 0), stop=(d == 1))
                ins.then_inc(s_Y, 1)

            pe.wait_ge(s_set, 10)
            pe.wait_ge(s_mod, 4)
            pe.wait_ge(s_cT, 2)
            pe.wait_ge(s_exps, 3)
            cb(0)
            states(0)
            cum_rows(0)
            for s in range(4 * NG):
                if s + 1 < 4 * NG:
                    cum_rows(s + 1)
                y_off(s)
                y_diag(s)
                if s % 4 == 3 and s // 4 + 1 < NG:
                    cb(s // 4 + 1)
                    states(s // 4 + 1)

            pe.wait_ge(s_E, 16 * NG)
            for b in range(16):
                u = units["z"][b // 2]
                arrived(pe, u)
                if b >= 4:
                    pe.wait_ge(s_sz, b - 3)
                w = slot(u)
                for i in range(2):
                    t = 2 * (b % 2) + i
                    for k in range(KD):
                        ins = pe.matmul(ps[:, b % 4, i * UC:(i + 1) * UC], aT[:, k, t * P:(t + 1) * P], w[:, k, :],
                                        start=(k == 0), stop=(k == KD - 1))
                ins.then_inc(s_z, 1)

            pe.wait_ge(s_yn, NT)
            for k in range(KI):
                if k >= 4:
                    if k % 2:
                        pe.wait_ge(s_yta, (k - 4) // 2 + 1)
                    else:
                        pe.wait_ge(s_ytd, (k - 4) // 2 + 1)
                for t in range(NT):
                    ins = pe.transpose(ps[:, 4 + k % 4, t * P:(t + 1) * P], xs[:, t, k * P:(k + 1) * P], ident)
                ins.then_inc(s_yt, 1)
            pe.wait_ge(s_sz, 16)
            for m in range(KD):
                u = units["out"][m]
                arrived(pe, u)
                if m >= 4:
                    pe.wait_ge(s_h1, m - 3)
                w = slot(u, KI)
                for k in range(KI):
                    if m == 0:
                        if k % 2:
                            pe.wait_ge(s_yta, k // 2 + 1)
                        else:
                            pe.wait_ge(s_ytd, k // 2 + 1)
                    ins = pe.matmul(ps[:, m % 4, :], w[:, k, :], yT[:, k, :], start=(k == 0), stop=(k == KI - 1))
                ins.then_inc(s_op, 1)

            def moe_pe(l):
                n = TOK[l]
                nt = n // P
                for t in range(nt):
                    for k in range(KD):
                        if t == 0:
                            pe.wait_ge(s_a, KD * (2 * l + 1) + k + 1)
                        ins = pe.matmul(ps[:, 6, t * NE:(t + 1) * NE], aT[:, k, t * P:(t + 1) * P], rw[:, k, :],
                                        start=(k == 0), stop=(k == KD - 1))
                ins.then_inc(s_rl, 1)

                C = CAP[l]
                w = [units[f"moe{l}"][j] for j in range(6)]

                def hidden_chunk(e, f):
                    q = KF * e + f
                    if f % 2 == 0:
                        arrived(pe, w[f], e)
                        arrived(pe, w[f + 1], e)
                    if not (isinstance(e, int) and q < 2):
                        pe.wait_ge(s_hid[l], q - 1)
                    for r in range(2):
                        ws = slot(w[2 * (f // 2) + r])
                        for k in range(KD):
                            ins = pe.matmul(ps[:, 2 * (f % 2) + r, 0:n], ws[:, k, (f % 2) * P:(f % 2 + 1) * P],
                                            aT[:, k, 0:n], start=(k == 0), stop=(k == KD - 1))
                        if r == 1:
                            ins.then_inc(s_gu[l], 1)
                        elif f % 2 == 1:
                            ins.then_inc(s_gf[l], 1)

                def down(e):
                    first = isinstance(e, int)
                    arrived(pe, w[4], e)
                    arrived(pe, w[5], e)
                    for r in range(NOUT[l]):
                        t, c = r // 2, r % 2
                        y = NOUT[l] * e + r
                        if not (first and y < 4):
                            pe.wait_ge(s_yu[l], y - 3)
                        for k in range(KF):
                            if r == 0 and k % 3 == 0:
                                pe.wait_ge(s_hid[l], KF * e + (3 if k == 0 else 4))
                            ins = pe.matmul(ps[:, 4 + r % 4, :], hid[:, k, t * P:(t + 1) * P],
                                            slot(w[4 + k // 2], 2)[:, k % 2, c * 512:(c + 1) * 512],
                                            start=(k == 0), stop=(k == KF - 1))
                            if r == NOUT[l] - 1 and k == 1:
                                ins.then_inc(s_y4[l], 1)
                        ins.then_inc(s_yn4[l], 1)

                def turn_rows(n_in):
                    pe.wait_ge(s_gx[l], n_in)
                    for k in range(KD):
                        ins = pe.transpose(ps[:, 6 + k // 4, (k % 4) * C:(k % 4 + 1) * C], Xg[0:C, k * P:(k + 1) * P],
                                           ident[0:C, 0:C])
                    ins.then_inc(s_xt[l], 1)

                def sparse_expert(e):
                    pe.wait_ge(s_xa[l], e + 1)
                    pe.wait_ge(s_xd[l], e + 1)
                    for p in range(2):
                        arrived(pe, w[2 * p], e + 1)
                        arrived(pe, w[2 * p + 1], e + 1)
                        pe.wait_ge(s_hid2[l], 2 * e + p + 1)
                        for f in range(2):
                            for r in range(2):
                                ws = slot(w[2 * p + r])
                                for k in range(KD):
                                    ins = pe.matmul(ps[:, 2 * p + r, f * C:(f + 1) * C], ws[:, k, f * P:(f + 1) * P],
                                                    XgT[:, k * C:(k + 1) * C], start=(k == 0), stop=(k == KD - 1))
                                if f == 1:
                                    ins.then_inc((s_gf2, s_gu2)[r][l], 1)
                    turn_rows(16 * e + 32)
                    arrived(pe, w[4], e + 1)
                    arrived(pe, w[5], e + 1)
                    pe.wait_ge(s_ya[l], e + 1)
                    pe.wait_ge(s_yd[l], e + 1)
                    for c in range(2):
                        for k in range(KF):
                            if c == 0 and k % 2 == 0:
                                pe.wait_ge(s_hid2[l], 2 * e + 3 + k // 2)
                            ins = pe.matmul(ps[0:C, 4 + c, :], hidS[:, k, :], slot(w[4 + k // 2], 2)[:, k % 2, c * 512:(c + 1) * 512],
                                            start=(k == 0), stop=(k == KF - 1))
                            if c == 1 and k == 1:
                                ins.then_inc(s_y42[l], 1)
                        ins.then_inc(s_dn[l], 1)

                def turn_sum(ready):
                    for t in range(nt):
                        ready(t)
                        for k in range(KD):
                            ins = pe.transpose(ps[:, k, t * P:(t + 1) * P], acc[:, t, k * P:(k + 1) * P], ident)
                            if t == nt - 1:
                                ins.then_inc(s_mt, 1)

                hidS = hid_s(C)
                hidden_chunk(0, 0)
                for r in range(2 * nt):
                    if r >= 2:
                        pe.wait_ge(s_mtv, 8 * l + r - 1)
                    for k in range(4):
                        kk = 4 * (r % 2) + k
                        ins = pe.transpose(ps[:, (4, 7)[r % 2], k * P:(k + 1) * P], aT[:, kk, (r // 2) * P:(r // 2 + 1) * P], ident)
                    ins.then_inc(s_mt8, 1)
                hidden_chunk(0, 1)
                pe.wait_ge(s_sel, 1 * l + 1)
                sel = [rt[12][:, t * NE:(t + 1) * NE] for t in range(nt)]
                for t in range(nt):
                    for q in range(t + 1):
                        pe.matmul(ps[:, 6, t * NE:(t + 1) * NE], tri_f if q == t else ones[:, :], sel[q],
                                  start=(q == 0), stop=(q == t))
                for q in range(nt):
                    ins = pe.matmul(ps[:, 6, 64:64 + NE], ones[:, :], sel[q], start=(q == 0), stop=(q == nt - 1))
                ins.then_inc(s_rk, 1)
                hidden_chunk(0, 2)
                pe.wait_ge(s_oh, 4 * l + nt)
                pe.wait_ge(s_val, 18 * l + 18)
                for e in range(NE):
                    for t in range(nt):
                        ins = pe.matmul(ps[0:C, 5, 3 * e:3 * e + 3], onehot[:, t, e, 0:C], val[:, t, e, :],
                                        start=(t == 0), stop=(t == nt - 1))
                ins.then_inc(s_ix, 1)
                hidden_chunk(0, 3)
                pe.wait_ge(s_mtv, 8 * l + 2 * nt)
                pe.wait_ge(s_gi, 3 * l + 1)
                down(0)
                sparse = choose(pe, l)
                with pe.If(sparse):
                    pe.wait_ge(s_yu[l], NOUT[l])
                    turn_rows(16)
                    with pe.Fori(0, NE) as e:
                        sparse_expert(e)
                    turn_sum(lambda t: pe.wait_ge(s_acc[l], 2 * t + 2))
                with pe.Else():
                    with pe.Fori(0, NE) as e:
                        for f in range(KF):
                            hidden_chunk(e + 1, f)
                        down(e + 1)
                    pe.wait_ge(s_mr, 16 * (l + 1))
                    pe.wait_ge(s_yf[l], 2)
                    turn_sum(lambda t: pe.wait_ge(s_yu[l], NOUT[l] * (NE + 1)))

            pe.wait_ge(s_ytd, 8)
            pe.wait_ge(s_yta, 8)
            mean_square(1, T, 7)
            moe_pe(0)

            pe.wait_ge(s_h2, KD)
            mean_square(2, T, 7)
            pe.wait_ge(s_a, 3 * KD)
            for c in range(4):
                u = units["q"][c]
                arrived(pe, u)
                w = slot(u)
                for r in range(2):
                    for k in range(KD):
                        ins = pe.matmul(ps[:, c, r * S:(r + 1) * S], w[:, k, r * P:(r + 1) * P], aT[:, k, 0:S],
                                        start=(k == 0), stop=(k == KD - 1))
                ins.then_inc(s_q, 1)
            arrived(pe, units["k"][0])
            w = slot(units["k"][0])
            for m in range(2):
                for k in range(KD):
                    ins = pe.matmul(ps[:, 4 + m, :], w[:, k, m * P:(m + 1) * P], aT[:, k, :],
                                    start=(k == 0), stop=(k == KD - 1))
            ins.then_inc(s_kv, 1)
            arrived(pe, units["v"][0])
            pe.wait_ge(s_rs, 6)
            w = slot(units["v"][0])
            for t in range(NT):
                for k in range(KD):
                    ins = pe.matmul(ps[:, 6 + t // 2, (t % 2) * UC:(t % 2 + 1) * UC], aT[:, k, t * P:(t + 1) * P],
                                    w[:, k, :], start=(k == 0), stop=(k == KD - 1))
                if t % 2:
                    ins.then_inc(s_kv, 1)
            for c in range(4):
                pe.wait_ge(s_qc, c + 1)
                pe.matmul(ps[:, c, :], rope_m, QT[:, 2 * c:2 * c + 2, :], start=True, stop=True).then_inc(s_rot, 1)
            pe.wait_ge(s_kc, 2)
            pe.matmul(ps[:, 4, :].rearrange("p (c n) -> p c n", c=2), rope_m, KT[:, :, 0:S], start=True, stop=True)\
                .then_inc(s_rot, 1)
            pe.wait_ge(s_rp, 5)
            pe.wait_ge(s_kx, 32)
            pe.wait_ge(s_vv, 2)

            def scores(n):
                b, h = divmod(n, QH)
                kv = h // 4
                lo = slice((h % 2) * HD, (h % 2 + 1) * HD)
                keys = KT if kv % 2 == h % 2 else KX
                if n >= 2:
                    pe.wait_ge(s_p, n - 1)
                pe.matmul(ps[:, n % 2, :], identb, amask[b], start=True, stop=False)
                pe.matmul(ps[:, n % 2, :], QT[lo, h // 2, b * P:(b + 1) * P], keys[lo, kv // 2, :], start=False, stop=True)\
                    .then_inc(s_sc, 1)

            def turn_probs(n):
                pe.wait_ge(s_p, n + 1)
                if n >= 2:
                    pe.wait_ge(s_ptv, n - 1)
                for j in range(NT):
                    ins = pe.transpose(ps[:, 2 + n % 2, j * P:(j + 1) * P], pr[n % 2][:, j * P:(j + 1) * P], ident)
                ins.then_inc(s_pt, 1)

            def pv(n):
                b, h = divmod(n, QH)
                kv = h // 4
                pe.wait_ge(s_ptv, n + 1)
                for j in range(NT):
                    ins = pe.matmul(ps[:, 4 + 2 * b + h // 8, (h % 8) * HD:(h % 8 + 1) * HD], prT[n % 2][:, j * P:(j + 1) * P],
                                    V[:, j, kv * HD:(kv + 1) * HD], start=(j == 0), stop=(j == NT - 1))
                ins.then_inc(s_pv, 1)

            for n in range(34):
                if n < 32:
                    scores(n)
                if 1 <= n < 33:
                    turn_probs(n - 1)
                if n >= 2:
                    pv(n - 2)
            pe.wait_ge(s_o, 4)
            for k in range(8):
                for t in range(2):
                    ins = pe.transpose(ps[:, k // 2, (k % 2) * S + t * P:(k % 2) * S + (t + 1) * P],
                                       O[:, t, k * P:(k + 1) * P], ident)
                if k % 2:
                    ins.then_inc(s_ot, 1)
            for m in range(KD):
                u = units["ao"][m // 2]
                arrived(pe, u)
                if m >= 4:
                    pe.wait_ge(s_h1, KD + m - 3)
                w = slot(u)
                for k in range(8):
                    if m == 0 and k % 2 == 0:
                        pe.wait_ge(s_otv, k // 2 + 1)
                    ins = pe.matmul(ps[:, 4 + m % 4, 0:S], w[:, k, (m % 2) * P:(m % 2 + 1) * P], oT[:, k, :],
                                    start=(k == 0), stop=(k == 7))
                ins.then_inc(s_ao, 1)
            mean_square(3, S, 0)
            pe.wait_ge(s_h1, 2 * KD)
            pe.wait_ge(s_rs, 8)
            moe_pe(1)
            for t in range(2):
                for c in range(2):
                    pe.wait_ge(s_h2, 2 * KD)
                    for k in range(4):
                        ins = pe.transpose(ps[:, 2 * t + c, k * P:(k + 1) * P], hT[:, 4 * c + k, t * P:(t + 1) * P], ident)
                    ins.then_inc(s_ft, 1)

        @block.vector
        def _(dve):
            chain = [0]

            def link(ins):
                chain[0] += 1
                ins.then_inc(s_v, 1)
                dve.wait_ge(s_v, chain[0])

            dve.wait_ge(s_pkT, 1)
            dve.tensor_copy(par[:, :], ps[:, 0, 0:312]).then_inc(s_par, 1)
            for k in range(0, KD, 2):
                dve.wait_ge(s_xT, k + 1)
                dve.tensor_copy(hT[:, k, :], ps[:, (k + 1) % 8, :]).then_inc(s_hd, 1)

            def modulation(l, bank):
                dve.wait_ge(s_ada, ADA_U * (l + 1))
                dve.tensor_tensor(mod[:, l, :, :], ps[:, bank, 0:96].rearrange("p (j c) -> p j c", c=2),
                                  par[:, P + 48 * l:P + 48 * (l + 1)].unsqueeze(2).to_broadcast([P, 48, 2]), ALU.add)\
                    .then_inc(s_mod, 1)
                dve.wait_ge(s_mod, 3 * l + 1)
                for m in range(2):
                    w = par[:, P + 96 + 16 * m + KD * l:P + 96 + 16 * m + KD * (l + 1)]
                    dve.scalar_tensor_tensor(out=amod[:, l, m, :, :], in0=mod[:, l, 8 + 24 * m:16 + 24 * m, :], scalar=1.0,
                                             in1=w.unsqueeze(2).to_broadcast([P, KD, 2]), op0=ALU.add, op1=ALU.mult)\
                        .then_inc(s_mod, 1)

            def norm(i, n, bank):
                dve.wait_ge(s_ms, i + 1)
                link(dve.tensor_scalar(rstd[:, 0:n], ps[:, bank, 0:n], EPS, None, ALU.add))
                dve.reciprocal(rstd[:, 0:n], rstd[:, 0:n]).then_inc(s_rs, 1)
                dve.wait_ge(s_rs, 2 * i + 2)
                for k in range(KD):
                    dve.tensor_tensor(aT[:, k, 0:n], hT[:, k, 0:n], rstd[:, 0:n], ALU.mult).then_inc(s_nx, 1)

            norm(0, T, 7)
            modulation(0, 1)

            dve.wait_ge(s_bc, 16 * 7)
            dve.wait_ge(s_dt, 1)
            dve.tensor_tensor(sp[0].rearrange("p (t n) -> p t n", t=NT), ps[:, 5, 0:256].rearrange("p (t n) -> p t n", t=NT),
                              dtb[:, :].unsqueeze(1).to_broadcast([P, NT, 64]), ALU.add).then_inc(s_sp, 1)
            dve.wait_ge(s_sp, 1)
            link(dve.tensor_scalar(sp[7], sp[0], -1.0, None, ALU.mult))
            dve.tensor_tensor(sp[1], sp[0], sp[7], ALU.max).then_inc(s_sp, 1)
            dve.wait_ge(s_sp, 3)
            link(dve.tensor_scalar(sp[2], sp[1], 2.0, None, ALU.add))
            link(dve.reciprocal(sp[3], sp[2]))
            link(dve.tensor_tensor(sp[4], sp[1], sp[3], ALU.mult))
            link(dve.tensor_tensor(sp[5], sp[4], sp[4], ALU.mult))
            link(dve.tensor_scalar(sp[2], sp[5], 1.0 / 17, None, ALU.mult))
            for n in (15, 13, 11, 9, 7, 5, 3):
                link(dve.scalar_tensor_tensor(out=sp[2], in0=sp[2], scalar=1.0 / n, in1=sp[5], op0=ALU.add, op1=ALU.mult))
            link(dve.scalar_tensor_tensor(out=sp[2], in0=sp[2], scalar=1.0, in1=sp[4], op0=ALU.add, op1=ALU.mult))
            link(dve.tensor_scalar(sp[3], sp[0], 0.0, None, ALU.max))
            link(dve.scalar_tensor_tensor(out=dt[:, :, :].rearrange("p t n -> p (t n)"), in0=sp[2], scalar=2.0, in1=sp[3],
                                          op0=ALU.mult, op1=ALU.add))
            dve.wait_ge(s_sp, 4)
            dve.scalar_tensor_tensor(out=sp[6].rearrange("p (t n) -> p t n", t=NT), in0=dt[:, :, :], scalar=-1.0,
                                     in1=expa[:, :].unsqueeze(1).to_broadcast([P, NT, 64]), op0=ALU.mult, op1=ALU.mult)\
                .then_inc(s_sp, 1)

            def cum_copies():
                dve.wait_ge(s_cum, 1)
                dve.tensor_copy(cum[:, :, :].rearrange("p t n -> p (t n)"), ps[:, 6, 0:256]).then_inc(s_cumv, 1)
                dve.tensor_copy(cdec[:, :, :].rearrange("p t n -> p (t n)"), ps[:, 7, 0:256]).then_inc(s_cumv, 1)
                dve.wait_ge(s_cumv, 2)
                dve.tensor_tensor(wdt[:, :, :], cdec[:, :, :], cum[:, :, :], ALU.subtract).then_inc(s_cumv, 1)
                dve.tensor_scalar(ncum[:, :, :], cum[:, :, :], -1.0, None, ALU.mult).then_inc(s_cumv, 1)

            def conv(i):
                ch = i + KI if i < 8 else i - 8
                dve.wait_ge(s_pre, i + 1)
                if i >= 2:
                    dve.wait_ge(s_sil, i - 1)
                o = cacc[i % 2].rearrange("p (s n) -> p s n", s=2)
                link(dve.tensor_scalar(o, pre[i % 3][:, :, 0:S], par[:, ch:ch + 1], par[:, 272 + ch:273 + ch],
                                       ALU.mult, ALU.add))
                for tap in range(1, TAPS):
                    ins = dve.scalar_tensor_tensor(out=o, in0=pre[i % 3][:, :, tap:tap + S],
                                                   scalar=par[:, tap * NCONV + ch:tap * NCONV + ch + 1], in1=o,
                                                   op0=ALU.mult, op1=ALU.add)
                    if tap < TAPS - 1:
                        link(ins)
                ins.then_inc(s_conv, 1)

            for i in range(NCONV):
                conv(i)
                if i == 7:
                    cum_copies()
                if i == 12:
                    dve.wait_ge(s_cT, 1)
                    dve.tensor_copy(cumT[:, :], ps[0:64, 5, :]).then_inc(s_cT, 1)
            modulation(1, 0)
            dve.wait_ge(s_exps, 3)
            dve.tensor_tensor(wdt[:, :, :], wdt[:, :, :], dt[:, :, :], ALU.mult).then_inc(s_wdt, 1)

            def heads(v, col):
                return v[:, col:col + HG].unsqueeze(2).to_broadcast([P, HG, HP])

            def per_head(v):
                return v.rearrange("p (h n) -> p h n", h=HG)

            def take_states(g):
                dve.wait_ge(s_b4, 7 * g + 1)
                dve.tensor_copy(cbs[g % 2], ps[:, 4, :]).then_inc(s_b4v, 1)
                for q, (d, t) in enumerate([(0, 2), (1, 3), (0, 3), (1, 2), (0, 0), (1, 1)]):
                    n = q // 2
                    if n == 0:
                        dve.wait_ge(s_b4, 7 * g + q + 2)
                        dve.tensor_copy(H[d][0], ps[:, 4, :]).then_inc(s_b4v, 1)
                    else:
                        dve.wait_ge(s_b4v, 7 * g + q)
                        link(dve.tensor_tensor(per_head(H[d][n]), per_head(H[d][n - 1]),
                                               heads(cdec[:, t, :], d * NH + g * HG), ALU.mult))
                        dve.wait_ge(s_b4, 7 * g + q + 2)
                        dve.tensor_tensor(H[d][n], H[d][n], ps[:, 4, :], ALU.add).then_inc(s_b4v, 1)

            for s in range(4 * NG):
                g, t = s // 4, TILE_ORDER[s % 4]
                cg = g * HG
                if s % 4 == 0:
                    take_states(g)
                for d in range(2):
                    dve.wait_ge(s_E, 4 * s + 2 * d + 2)
                    m = E[:, s % 2, d * HG:(d + 1) * HG, :]
                    if d == 0 and s % 4 == 0:
                        dve.wait_ge(s_b4v, 7 * g + 1)
                    dve.tensor_tensor(m, m, cbs[g % 2][:, t * P:(t + 1) * P].unsqueeze(1).to_broadcast([P, HG, P]),
                                      ALU.mult).then_inc(s_M, 1)
                dve.wait_ge(s_off, s + 1)
                if s >= 2:
                    dve.wait_ge(s_y, s - 1)
                y = yb[s % 2]
                if t == 2:
                    link(dve.tensor_tensor(per_head(y), per_head(ps[:, 7, :]), heads(ecum[:, t, :], NH + cg), ALU.mult))
                elif t == 3:
                    link(dve.tensor_tensor(per_head(y), per_head(ps[:, 6, :]), heads(ecum[:, t, :], cg), ALU.mult))
                else:
                    dve.tensor_tensor(per_head(y), per_head(ps[:, 6, :]), heads(ecum[:, t, :], cg), ALU.mult)
                    link(dve.tensor_tensor(per_head(rstd[:, :]), per_head(ps[:, 7, :]), heads(ecum[:, t, :], NH + cg),
                                           ALU.mult))
                    link(dve.tensor_tensor(y, y, rstd[:, :], ALU.add))
                dve.wait_ge(s_Y, s + 1)
                dve.tensor_tensor(y, y, ps[:, 5, :], ALU.add).then_inc(s_yo, 1)

            dve.wait_ge(s_y, 4 * NG)
            for b in range(16):
                t = 2 * (b % 2)
                dve.wait_ge(s_sz, b + 1)
                yv = xs[:, t:t + 2, (b // 2) * UC:(b // 2 + 1) * UC]
                dve.tensor_tensor(yv, yv, sz[b % 2].rearrange("p (t n) -> p t n", t=2), ALU.mult).then_inc(s_zy, 1)
            dve.wait_ge(s_ss, NT)
            link(dve.tensor_scalar(small[:, 12:16], small[:, 0:4], 1.0 / DI, EPS, ALU.mult, ALU.add))
            dve.reciprocal(small[:, 4:8], small[:, 12:16]).then_inc(s_ss, 1)
            dve.wait_ge(s_ss, NT + 2)
            dve.wait_ge(s_zy, 16)
            for t in range(NT):
                dve.tensor_scalar(xs[:, t, :], xs[:, t, :], small[:, 8 + t:9 + t], None, ALU.mult).then_inc(s_yn, 1)
            for k in range(0, KI, 2):
                dve.wait_ge(s_yt, k + 1)
                dve.tensor_scalar(yT[:, k, :], ps[:, 4 + k % 4, :], par[:, 256 + k:257 + k], None, ALU.mult)\
                    .then_inc(s_ytd, 1)
            for m in range(KD):
                dve.wait_ge(s_op, m + 1)
                for q in range(2):
                    ins = dve.scalar_tensor_tensor(out=hT[:, m, q * S:(q + 1) * S], in0=ps[:, m % 4, q * S:(q + 1) * S],
                                                   scalar=mod[:, 0, 16 + m, q:q + 1], in1=hT[:, m, q * S:(q + 1) * S],
                                                   op0=ALU.mult, op1=ALU.add)
                ins.then_inc(s_h1, 1)

            def route(l):
                nt = TOK[l] // P
                n = nt * NE

                def v(i, m=n):
                    return rt[i][:, 0:m]

                def e3(i):
                    return rt[i][:, 0:n].rearrange("p (t e) -> p t e", e=NE)

                def g4(i):
                    return rt[i][:, 0:n].rearrange("p (g e) -> p g e", e=4)

                def tg(i):
                    return rt[i][:, 0:4 * nt].rearrange("p (t g) -> p t g", g=4)

                dve.wait_ge(s_rs1, l + 1)
                link(dve.tensor_tensor(e3(1), e3(0), rb[:, :].unsqueeze(1).to_broadcast([P, nt, NE]), ALU.add))
                b = g4(1)
                gs, pair = rt[2][:, 0:4 * nt], rt[3][:, 0:4 * nt]
                first = True
                for i in range(4):
                    for j in range(i + 1, 4):
                        o = gs if first else pair
                        link(dve.tensor_tensor(o.unsqueeze(2), b[:, :, i:i + 1], b[:, :, j:j + 1], ALU.add))
                        if not first:
                            link(dve.tensor_tensor(gs, gs, pair, ALU.max))
                        first = False
                best, eq = rt[4][:, 0:nt], tg(5)
                link(dve.tensor_reduce(best, tg(2), AX.X, ALU.max))
                link(dve.tensor_tensor(eq, tg(2), best.unsqueeze(2).to_broadcast([P, nt, 4]), ALU.is_equal))
                link(dve.tensor_tensor(eq, eq, erev[:, NE:NE + 4].unsqueeze(1).to_broadcast([P, nt, 4]), ALU.mult))
                link(dve.tensor_reduce(best, eq, AX.X, ALU.max))
                link(dve.tensor_tensor(eq, eq, best.unsqueeze(2).to_broadcast([P, nt, 4]), ALU.is_equal))
                gm = rt[5][:, 0:4 * nt].unsqueeze(2).to_broadcast([P, 4 * nt, 4])
                link(dve.tensor_tensor(g4(6), b, gm, ALU.mult))
                link(dve.tensor_scalar(rt[7][:, 0:4 * nt], rt[5][:, 0:4 * nt], -1.0, -NEG, ALU.add, ALU.mult))
                link(dve.tensor_tensor(g4(6), g4(6), rt[7][:, 0:4 * nt].unsqueeze(2).to_broadcast([P, 4 * nt, 4]), ALU.add))
                for i in range(2):
                    o = 8 + i
                    link(dve.tensor_reduce(best, e3(6), AX.X, ALU.max))
                    link(dve.tensor_tensor(e3(o), e3(6), best.unsqueeze(2).to_broadcast([P, nt, NE]), ALU.is_equal))
                    link(dve.tensor_tensor(e3(o), e3(o), erev[:, 0:NE].unsqueeze(1).to_broadcast([P, nt, NE]), ALU.mult))
                    link(dve.tensor_reduce(best, e3(o), AX.X, ALU.max))
                    link(dve.tensor_tensor(e3(o), e3(o), best.unsqueeze(2).to_broadcast([P, nt, NE]), ALU.is_equal))
                    if i == 0:
                        link(dve.scalar_tensor_tensor(out=v(6), in0=v(8), scalar=NEG, in1=v(6), op0=ALU.mult, op1=ALU.add))
                dve.tensor_tensor(v(12), v(8), v(9), ALU.add).then_inc(s_sel, 1)
                wl = wk[:, :, 0:nt]
                for i in range(2):
                    link(dve.tensor_tensor(v(10 + i), v(8 + i), v(0), ALU.mult))
                    link(dve.tensor_reduce(wl[:, i, :], e3(10 + i), AX.X, ALU.add))
                link(dve.tensor_tensor(best, wl[:, 0, :], wl[:, 1, :], ALU.add))
                link(dve.reciprocal(rt[13][:, 0:nt], best))
                link(dve.tensor_tensor(wl, wl, rt[13][:, 0:nt].unsqueeze(1).to_broadcast([P, 2, nt]), ALU.mult))
                dve.wait_ge(s_sel, 1 * l + 1)
                link(dve.tensor_tensor(v(8), v(12), v(0), ALU.mult))
                link(dve.tensor_tensor(comb[:, 0:nt, :], e3(8), rt[13][:, 0:nt].unsqueeze(2).to_broadcast([P, nt, NE]),
                                       ALU.mult))

            def place(l):
                nt, C = TOK[l] // P, CAP[l]
                dve.wait_ge(s_rk, 1 * l + 1)
                link(dve.tensor_tensor(rank[:, 0:nt * NE], ps[:, 6, 0:nt * NE], rt[12][:, 0:nt * NE], ALU.mult))
                for t in range(nt):
                    dve.tensor_tensor(onehot[:, t, :, 0:C], iota1[:, 0:C].unsqueeze(1).to_broadcast([P, NE, C]),
                                      rank[:, t * NE:(t + 1) * NE].unsqueeze(2).to_broadcast([P, NE, C]), ALU.is_equal)\
                        .then_inc(s_oh, 1)
                link(dve.tensor_reduce(sl[0][0:1, 0:1], ps[0:1, 6, 64:64 + NE], AX.X, ALU.max))
                dve.tensor_scalar(flag[0:1, 0:1], sl[0][0:1, 0:1], float(C), None, ALU.is_gt).then_inc(s_flag, 1)

            def indices(l):
                C = CAP[l]
                dve.wait_ge(s_ix, 1 * l + 1)
                dve.tensor_copy(slots[0:C, :, :], ps[0:C, 5, 0:3 * NE].rearrange("p (e v) -> p e v", e=NE)).then_inc(s_gi, 1)
                dve.wait_ge(s_gi, 3 * l + 1)
                f, emp, row, k512 = (sl[n][0:C, :].unsqueeze(2) for n in range(4))
                link(dve.scalar_tensor_tensor(out=f, in0=slots[0:C, :, 1:2], scalar=float(P), in1=slots[0:C, :, 0:1],
                                              op0=ALU.mult, op1=ALU.add))
                link(dve.tensor_scalar(emp, f, 0.0, float(EMPTY), ALU.is_equal, ALU.mult))
                link(dve.scalar_tensor_tensor(out=row, in0=f, scalar=-float(P), in1=emp, op0=ALU.add, op1=ALU.add))
                dve.tensor_copy(gidx[0:C, 0:NE], sl[2][0:C, :]).then_inc(s_gi, 1)
                dve.scalar_tensor_tensor(out=sidx[0:C, 0:NE].unsqueeze(2), in0=slots[0:C, :, 2:3], scalar=float(T), in1=row,
                                         op0=ALU.mult, op1=ALU.add).then_inc(s_gi, 1)

            def moe_dve(l):
                n = TOK[l]
                nt, C = n // P, CAP[l]
                hidS = hid_s(C)

                def chunk(e, f):
                    dve.wait_ge(s_sg[l], KF * e + f + 1)
                    dve.tensor_tensor(hid[:, f, 0:n], sg[f % 2][:, 0:n], ps[:, 2 * (f % 2) + 1, 0:n], ALU.mult)\
                        .then_inc(s_hid[l], 1)

                def outputs(e, w):
                    for r in range(NOUT[l]):
                        t, c = r // 2, r % 2
                        y = NOUT[l] * e + r
                        dve.wait_ge(s_yn4[l], y + 1)
                        o = acc[:, t, c * 512:(c + 1) * 512]
                        if w is None:
                            dve.tensor_copy(o, ps[:, 4 + r % 4, :]).then_inc(s_yu[l], 1)
                        else:
                            dve.wait_ge(s_yu[l], y - NOUT[l] + 1)
                            dve.scalar_tensor_tensor(out=o, in0=ps[:, 4 + r % 4, :], scalar=w[:, t, :],
                                                     in1=o, op0=ALU.mult, op1=ALU.add).then_inc(s_yu[l], 1)

                route(l)
                dve.wait_ge(s_val, 18 * l + 17)
                dve.tensor_copy(val[:, 0:nt, :, 2:3], rt[9][:, 0:nt * NE].rearrange("p (t e v) -> p t e v", e=NE, v=1))\
                    .then_inc(s_val, 1)
                chunk(0, 0)
                chunk(0, 1)
                place(l)
                chunk(0, 2)
                indices(l)
                chunk(0, 3)
                outputs(0, None)
                dve.memset(mark[:, 2 + l:3 + l], 0.0).then_inc(s_hid2[l], 2)
                dve.memset(mark[:, 4 + l:5 + l], 0.0).then_inc(s_yd[l], 1)
                sparse = choose(dve, l)
                with dve.If(sparse):
                    dve.wait_ge(s_xt[l], 1)
                    dve.tensor_copy(XgT[:, 4 * C:8 * C], ps[:, 7, 0:4 * C]).then_inc(s_xd[l], 1)
                    with dve.Fori(0, NE, 2) as e2:
                        for b in range(2):
                            e = e2 + b
                            for p in range(2):
                                dve.wait_ge(s_sg2[l], 2 * e + p + 1)
                                dve.tensor_tensor(hidS[:, 2 * p:2 * p + 2, :].rearrange("p k n -> p (k n)"), sg[p][:, 0:2 * C],
                                                  ps[:, 2 * p + 1, 0:2 * C], ALU.mult).then_inc(s_hid2[l], 1)
                            dve.wait_ge(s_xt[l], e + 2)
                            dve.tensor_copy(XgT[:, 4 * C:8 * C], ps[:, 7, 0:4 * C]).then_inc(s_xd[l], 1)
                            dve.wait_ge(s_dn[l], 2 * e + 2)
                            dve.wait_ge(s_yf[l], e + 1)
                            dve.tensor_copy(Y[b][0:C, 512:1024], ps[0:C, 5, :]).then_inc(s_yd[l], 1)
                    dve.wait_ge(s_yu[l], NOUT[l])
                    for t in range(nt):
                        dve.wait_ge(s_yp[l][t], 16)
                        for k in range(2):
                            if k:
                                dve.wait_ge(s_acc[l], 2 * t + 1)
                            dve.scalar_tensor_tensor(out=acc[:, t, :], in0=ypair[:, t, k, :], scalar=wk[:, k, t:t + 1],
                                                     in1=acc[:, t, :], op0=ALU.mult, op1=ALU.add).then_inc(s_acc[l], 1)
                with dve.Else():
                    with dve.Fori(0, NE) as e:
                        w = comb[:, :, bass.ds(e, 1)]
                        for f in range(KF):
                            chunk(e + 1, f)
                        outputs(e + 1, w)
                for k in range(KD):
                    dve.wait_ge(s_mt, KD * l + k + 1)
                    for q in range(n // S):
                        ins = dve.scalar_tensor_tensor(out=hT[:, k, q * S:(q + 1) * S], in0=ps[:, k, q * S:(q + 1) * S],
                                                       scalar=mod[:, l, 40 + k, q:q + 1], in1=hT[:, k, q * S:(q + 1) * S],
                                                       op0=ALU.mult, op1=ALU.add)
                    ins.then_inc(s_h2, 1)

            norm(1, T, 7)
            moe_dve(0)

            norm(2, T, 7)
            tabs = [v.unsqueeze(1).to_broadcast([P, 2, S]) for v in (cosT, sinT)]
            for c in range(5):
                x = QT[:, 2 * c:2 * c + 2, :] if c < 4 else KT[:, :, 0:S]
                rv = rq[c % 2].rearrange("p (c n) -> p c n", c=2)
                dve.wait_ge(s_rot, c + 1)
                if c >= 2:
                    dve.wait_ge(s_rp, c - 1)
                link(dve.tensor_tensor(rv, ps[:, c, :].rearrange("p (c n) -> p c n", c=2), tabs[1], ALU.mult))
                link(dve.tensor_tensor(x, x, tabs[0], ALU.mult))
                dve.tensor_tensor(x, x, rv, ALU.add).then_inc(s_rp, 1)
            for n in range(32):
                h = n % QH
                dve.wait_ge(s_sc, n + 1)
                dve.tensor_reduce(rmx[:, n:n + 1], ps[:, n % 2, :], AX.X, ALU.max).then_inc(s_mx, 1)
                dve.wait_ge(s_mx, 3 * n + 1)
                dve.tensor_scalar(mxa[:, n:n + 1], rmx[:, n:n + 1], SCALE, sink[:, h:h + 1], ALU.mult, ALU.max)\
                    .then_inc(s_mx, 1)
                dve.wait_ge(s_mx, 3 * n + 2)
                dve.tensor_scalar(nmx[:, n:n + 1], mxa[:, n:n + 1], -1.0, None, ALU.mult).then_inc(s_mx, 1)
            dve.tensor_tensor(esk.rearrange("p (b h) -> p b h", b=2), sink[:, :].unsqueeze(1).to_broadcast([P, 2, QH]),
                              mxa.rearrange("p (b h) -> p b h", b=2), ALU.subtract).then_inc(s_esk, 1)
            dve.wait_ge(s_esk, 2)
            link(dve.tensor_tensor(den, den, esk, ALU.add))
            link(dve.reciprocal(rden, den))
            dve.wait_ge(s_pv, 32)
            for n in range(4):
                b, c = n // 2, n % 2
                dve.tensor_tensor(O[:, b, c * 512:(c + 1) * 512].rearrange("p (h n) -> p h n", h=8),
                                  ps[:, 4 + n, :].rearrange("p (h n) -> p h n", h=8),
                                  rden[:, n * 8:(n + 1) * 8].unsqueeze(2).to_broadcast([P, 8, HD]), ALU.mult).then_inc(s_o, 1)
            for n in range(4):
                dve.wait_ge(s_ot, n + 1)
                dve.tensor_copy(oT[:, 2 * n:2 * n + 2, :], ps[:, n, :].rearrange("p (k n) -> p k n", k=2)).then_inc(s_otv, 1)
            for m in range(KD):
                dve.wait_ge(s_ao, m + 1)
                dve.scalar_tensor_tensor(out=hT[:, m, 0:S], in0=ps[:, 4 + m % 4, 0:S], scalar=mod[:, 1, 16 + m, 0:1],
                                         in1=hT[:, m, 0:S], op0=ALU.mult, op1=ALU.add).then_inc(s_h1, 1)
            norm(3, S, 0)
            moe_dve(1)

            for t in range(2):
                for c in range(2):
                    dve.wait_ge(s_ft, 2 * t + c + 1)
                    dve.tensor_copy(fin[:, t, c * 512:(c + 1) * 512], ps[:, 2 * t + c, :]).then_inc(s_fc, 1)
            dve.wait_ge(s_fs, 2)
            link(dve.tensor_scalar(small[:, 6:8], small[:, 0:2], 1.0 / D, EPS, ALU.mult, ALU.add))
            dve.reciprocal(small[:, 2:4], small[:, 6:8]).then_inc(s_fs, 1)
            dve.wait_ge(s_fs, 4)
            dve.wait_ge(s_fw, 16)
            for t in range(2):
                dve.scalar_tensor_tensor(out=fin[:, t, :], in0=fin[:, t, :], scalar=small[:, 4 + t:5 + t], in1=fnw,
                                         op0=ALU.mult, op1=ALU.mult).then_inc(s_fo, 1)


_INS = ["x", "c", "ctx", "c_ctx", "ada_w", "ada_b", "norm1_w", "norm2_w", "ssd_in_w", "ssd_conv_w", "ssd_conv_b",
        "ssd_dt_bias", "ssd_a_log", "ssd_d", "ssd_norm_w", "ssd_out_w", "attn_qkv_w", "attn_sink", "attn_out_w",
        "router_w", "router_bias", "moe_w_gate", "moe_w_up", "moe_w_down", "shared_w_gate", "shared_w_up",
        "shared_w_down", "final_norm_w"]


def kernel(**inputs):
    import concourse.bacc as bacc
    from concourse.bass_utils import run_bass_kernel_spmd

    nc = bacc.Bacc("TRN2", target_bir_lowering=False, num_devices=1)
    arrays = {n: np.ascontiguousarray(inputs[n]) for n in _INS}
    arrays["c32"], arrays["c16"], arrays["erev"], arrays["val"] = host_constants()
    aps = {n: nc.dram_tensor(f"in_{n}", v.shape, mybir.dt.from_np(v.dtype), kind="ExternalInput").ap()
           for n, v in arrays.items()}
    out = nc.dram_tensor("out", (1, S, D), F32, kind="ExternalOutput").ap()
    build(nc, aps, out)
    r = run_bass_kernel_spmd(nc, [{f"in_{n}": v for n, v in arrays.items()}], core_ids=[0])
    return r.results[0]["out"]
```
